# Optimizing a Trainium2 kernel written in Bass

```python
import math
import jax
import jax.numpy as jnp
from jax import lax
import numpy as np

D_MODEL = 1024
BATCH = 1
SEQ = 256
DEPTH = 1

N_MEM = 256
ATTN_GROUPS = ((128, 1), (512, 4), (2048, 16))
N_GROUPS = len(ATTN_GROUPS)
ATTN_HEADS = 8
HEAD_DIM = 64
ATTN_WIDTH = ATTN_HEADS * HEAD_DIM
Q_BLOCK = 128
CONV_WIDTH = D_MODEL
CONV_K = 3
ATTN_COLS = N_GROUPS * 3 * ATTN_WIDTH
IN_WIDTH = ATTN_COLS + 3 * CONV_WIDTH
N_BRANCHES = 2
MEM_HEADS = 4
MEM_HEAD_DIM = 128
MEM_WIDTH = MEM_HEADS * MEM_HEAD_DIM
N_EXPERTS = 32
TOP_K = 4
D_FF = D_MODEL
SWIGLU_LIMIT = 7.0
SWIGLU_ALPHA = 1.702
MOE_BLOCK = 128
EPS = 1e-6
NEG_INF = -1e30

kernel_name = "hybrid_dilated_attn_shortconv_moe"

def rms_norm(x, g):
    xf = x.astype(jnp.float32)
    y = xf * lax.rsqrt(jnp.mean(xf * xf, axis=-1, keepdims=True) + EPS)
    return (y * g.astype(jnp.float32)).astype(x.dtype)

def alibi_slopes(n_heads):
    return jnp.power(2.0, -8.0 * jnp.arange(1, n_heads + 1, dtype=jnp.float32) / n_heads)

def dilated_window_attention(q, k, v, window, dilation, slopes):
    B, S, H, Dh = q.shape
    L = S // dilation
    w_sub = window // dilation
    nb = -(-L // Q_BLOCK)
    Lp = nb * Q_BLOCK

    def to_blocks(a):
        a = a.reshape(B, L, dilation, H, Dh).transpose(0, 2, 1, 3, 4)
        a = jnp.pad(a, ((0, 0), (0, 0), (0, Lp - L), (0, 0), (0, 0)))
        return a.reshape(B, dilation, nb, Q_BLOCK, H, Dh)

    def with_prev(a):
        prev = jnp.pad(a[:, :, :-1], ((0, 0), (0, 0), (1, 0), (0, 0), (0, 0), (0, 0)))
        return jnp.concatenate([prev, a], axis=3)

    qb, kb, vb = to_blocks(q), to_blocks(k), to_blocks(v)
    kk, vv = with_prev(kb), with_prev(vb)
    s = jnp.einsum('brnqhd,brnkhd->brnhqk', qb, kk).astype(jnp.float32) * (Dh ** -0.5)
    iq = jnp.arange(Q_BLOCK)
    ik = jnp.arange(2 * Q_BLOCK)
    dist = iq[:, None] + Q_BLOCK - ik[None, :]
    key_ok = (jnp.arange(nb)[:, None] * Q_BLOCK + ik[None, :] - Q_BLOCK) >= 0
    mask = ((dist >= 0) & (dist <= w_sub))[None] & key_ok[:, None, :]
    bias = -slopes[:, None, None] * (dist * dilation).astype(jnp.float32)[None]
    s = jnp.where(mask[None, None, :, None], s + bias[None, None, None], NEG_INF)
    lse = jax.nn.logsumexp(s, axis=-1)
    p = jnp.exp(s - lse[..., None])
    o = jnp.einsum('brnhqk,brnkhd->brnqhd', p.astype(v.dtype), vv)
    o = o.reshape(B, dilation, Lp, H, Dh)[:, :, :L].transpose(0, 2, 1, 3, 4).reshape(B, S, H, Dh)
    lse = lse.transpose(0, 1, 2, 4, 3).reshape(B, dilation, Lp, H)[:, :, :L]
    lse = lse.transpose(0, 2, 1, 3).reshape(B, S, H)
    return o, lse

def short_conv_causal(z, conv_w):
    S = z.shape[1]
    zp = jnp.pad(z, ((0, 0), (CONV_K - 1, 0), (0, 0)))
    return sum(zp[:, k:k + S] * conv_w[k] for k in range(CONV_K))

def hybrid_mixer(u, w_in, conv_w, w_branch_attn, w_branch_conv, w_gate, b_gate, w_out):
    B, S, _ = u.shape
    proj = u @ w_in
    attn_cols, conv_cols = proj[..., :ATTN_COLS], proj[..., ATTN_COLS:]
    slopes = alibi_slopes(ATTN_HEADS)
    outs, lses = [], []
    for g, (window, dil) in enumerate(ATTN_GROUPS):
        cols = attn_cols[..., g * 3 * ATTN_WIDTH:(g + 1) * 3 * ATTN_WIDTH]
        cols = cols.reshape(B, S, 3, ATTN_HEADS, HEAD_DIM)
        o, lse = dilated_window_attention(cols[:, :, 0], cols[:, :, 1], cols[:, :, 2], window, dil, slopes)
        outs.append(o)
        lses.append(lse)
    wts = jax.nn.softmax(jnp.stack(lses), axis=0)
    y_attn = jnp.einsum('gbsh,gbshd->bshd', wts, jnp.stack(outs).astype(jnp.float32))
    y_attn = y_attn.reshape(B, S, ATTN_WIDTH).astype(u.dtype)
    gb, gc, xc = jnp.split(conv_cols, 3, axis=-1)
    y_conv = gb * short_conv_causal(gc * xc, conv_w)
    gates = jax.nn.sigmoid(u @ w_gate + b_gate)
    g_attn, g_conv = jnp.split(gates, N_BRANCHES, axis=-1)
    mixed = g_attn * (y_attn @ w_branch_attn) + g_conv * (y_conv @ w_branch_conv)
    return mixed @ w_out

def memory_cross_attention(u, m, w_cq, w_ckv, w_co):
    B, S, _ = u.shape
    q = (u @ w_cq).reshape(B, S, MEM_HEADS, MEM_HEAD_DIM)
    k, v = jnp.split((m @ w_ckv).reshape(B, m.shape[1], 2, MEM_HEADS, MEM_HEAD_DIM), 2, axis=2)
    k, v = k[:, :, 0], v[:, :, 0]
    s = jnp.einsum('bshd,bmhd->bhsm', q, k).astype(jnp.float32) * (MEM_HEAD_DIM ** -0.5)
    p = jax.nn.softmax(s, axis=-1)
    o = jnp.einsum('bhsm,bmhd->bshd', p.astype(v.dtype), v).reshape(B, S, MEM_WIDTH)
    return o @ w_co

def moe_ffn(u, router_w, router_b, w_eg, b_eg, w_eu, b_eu, w_ed, b_ed):
    T, D = u.shape
    logits = (u @ router_w + router_b).astype(jnp.float32)
    top_logit, top_idx = lax.top_k(logits, TOP_K)
    top_w = jax.nn.softmax(top_logit, axis=-1)
    n_assign = T * TOP_K
    flat_e = top_idx.reshape(-1)
    flat_tok = jnp.arange(n_assign, dtype=jnp.int32) // TOP_K
    order = jnp.argsort(flat_e)
    e_sorted = flat_e[order]
    tok_sorted = flat_tok[order]
    w_sorted = top_w.reshape(-1)[order]
    counts = jnp.bincount(flat_e, length=N_EXPERTS)
    padded = (counts + MOE_BLOCK - 1) // MOE_BLOCK * MOE_BLOCK
    start = jnp.cumsum(counts) - counts
    pend = jnp.cumsum(padded)
    pstart = pend - padded
    row = pstart[e_sorted] + jnp.arange(n_assign) - start[e_sorted]
    n_rows = (-(-n_assign // MOE_BLOCK)) * MOE_BLOCK + N_EXPERTS * MOE_BLOCK
    n_blocks = n_rows // MOE_BLOCK
    row_tok = jnp.full((n_rows,), T, jnp.int32).at[row].set(tok_sorted)
    block_expert = jnp.clip(jnp.searchsorted(pend, jnp.arange(n_blocks) * MOE_BLOCK, side='right'),
                            0, N_EXPERTS - 1)
    u_pad = jnp.concatenate([u, jnp.zeros((1, D), u.dtype)], axis=0)
    xb = u_pad[row_tok].reshape(n_blocks, MOE_BLOCK, D)

    def expert_block(args):
        xblk, e = args
        gate = jnp.minimum(xblk @ w_eg[e] + b_eg[e], SWIGLU_LIMIT)
        lin = jnp.clip(xblk @ w_eu[e] + b_eu[e], -SWIGLU_LIMIT, SWIGLU_LIMIT)
        hdn = gate * jax.nn.sigmoid(SWIGLU_ALPHA * gate) * (lin + 1.0)
        return hdn @ w_ed[e] + b_ed[e]

    y_rows = lax.map(expert_block, (xb, block_expert)).reshape(n_rows, D)
    y_assign = y_rows[row].astype(jnp.float32) * w_sorted[:, None]
    return jax.ops.segment_sum(y_assign, tok_sorted, num_segments=T).astype(u.dtype)

def setup_inputs(seed: int = 0) -> dict:
    key = jax.random.key(seed)
    ks = jax.random.split(key, 26)
    nrm = lambda k, shape, fan_in: jax.random.normal(k, shape, jnp.float32) * (fan_in ** -0.5)
    gain = lambda k, shape: 1.0 + 0.02 * jax.random.normal(k, shape, jnp.float32)
    small = lambda k, shape: 0.01 * jax.random.normal(k, shape, jnp.float32)
    L, D, E = DEPTH, D_MODEL, N_EXPERTS
    return {
        "x": jax.random.normal(ks[0], (BATCH, SEQ, D), jnp.float32),
        "mem": jax.random.normal(ks[1], (BATCH, N_MEM, D), jnp.float32),
        "norm_mix": gain(ks[2], (L, D)),
        "w_in": nrm(ks[3], (L, D, IN_WIDTH), D),
        "conv_w": nrm(ks[4], (L, CONV_K, CONV_WIDTH), CONV_K),
        "w_branch_attn": nrm(ks[5], (L, ATTN_WIDTH, D), ATTN_WIDTH),
        "w_branch_conv": nrm(ks[6], (L, CONV_WIDTH, D), CONV_WIDTH),
        "w_gate": nrm(ks[7], (L, D, N_BRANCHES * D), D),
        "b_gate": small(ks[8], (L, N_BRANCHES * D)),
        "w_out": nrm(ks[9], (L, D, D), D),
        "norm_cross": gain(ks[10], (L, D)),
        "norm_mem": gain(ks[11], (L, D)),
        "w_cq": nrm(ks[12], (L, D, MEM_WIDTH), D),
        "w_ckv": nrm(ks[13], (L, D, 2 * MEM_WIDTH), D),
        "w_co": nrm(ks[14], (L, MEM_WIDTH, D), MEM_WIDTH),
        "norm_moe": gain(ks[15], (L, D)),
        "router_w": nrm(ks[16], (L, D, E), D),
        "router_b": small(ks[17], (L, E)),
        "w_exp_gate": nrm(ks[18], (L, E, D, D_FF), D),
        "b_exp_gate": small(ks[19], (L, E, D_FF)),
        "w_exp_up": nrm(ks[20], (L, E, D, D_FF), D),
        "b_exp_up": small(ks[21], (L, E, D_FF)),
        "w_exp_down": nrm(ks[22], (L, E, D_FF, D), D_FF),
        "b_exp_down": small(ks[23], (L, E, D)),
        "norm_final": gain(ks[24], (D,)),
    }

def reference(x, mem, norm_mix, w_in, conv_w, w_branch_attn, w_branch_conv, w_gate, b_gate, w_out,
              norm_cross, norm_mem, w_cq, w_ckv, w_co, norm_moe, router_w, router_b,
              w_exp_gate, b_exp_gate, w_exp_up, b_exp_up, w_exp_down, b_exp_down, norm_final):
    B, S, D = x.shape
    h = x
    for l in range(DEPTH):
        u = rms_norm(h, norm_mix[l])
        h = h + hybrid_mixer(u, w_in[l], conv_w[l], w_branch_attn[l], w_branch_conv[l],
                             w_gate[l], b_gate[l], w_out[l])
        u = rms_norm(h, norm_cross[l])
        m = rms_norm(mem, norm_mem[l])
        h = h + memory_cross_attention(u, m, w_cq[l], w_ckv[l], w_co[l])
        u = rms_norm(h, norm_moe[l]).reshape(B * S, D)
        h = h + moe_ffn(u, router_w[l], router_b[l], w_exp_gate[l], b_exp_gate[l],
                        w_exp_up[l], b_exp_up[l], w_exp_down[l], b_exp_down[l]).reshape(B, S, D)
    return rms_norm(h, norm_final)


_drawn_inputs = setup_inputs


def setup_inputs(seed=0):
    import zlib

    import numpy as np

    out = dict(_drawn_inputs(seed))
    spreads = {}
    factors = {'b_gate': 3.524,
     'norm_cross': 8.0,
     'norm_mem': 3.294,
     'b_exp_gate': 37.405,
     'b_exp_up': 53.427,
     'b_exp_down': 34.773,
     'norm_final': 8.13,
     'norm_moe': 4.132,
     'router_b': 5.78}
    for name, (base, spread) in spreads.items():
        noise = np.random.default_rng([zlib.crc32(name.encode()), seed]).standard_normal(out[name].shape)
        drawn = base * np.exp(spread * noise) if base else spread * noise
        out[name] = jnp.asarray(drawn.astype(out[name].dtype))
    for name, factor in factors.items():
        out[name] = (out[name] * factor).astype(out[name].dtype)
    return out
```

```python
from contextlib import ExitStack

import numpy as np

import concourse.bass as bass
from concourse import mybir

F32 = mybir.dt.float32
I32 = mybir.dt.int32
ALU = mybir.AluOpType
ACT = mybir.ActivationFunctionType
AX_X = mybir.AxisListType.X

P = 128
T, D = 256, 1024
TT = T // P
DC = D // P
GROUPS, HEADS, HD = 3, 8, 64
AW = HEADS * HD
DILATION = (1, 4, 16)
WINDOW_STEPS = 128
PAIRS = HEADS // 2
CONV_K = 3
MH, MHD = 4, 128
E, TOPK, FF = 32, 4, 1024
SLOTS = 64
LIMIT, ALPHA, EPS = 7.0, 1.702, 1e-6
SENTINEL, TAKEN = -3.0e38, -3.3e38
MASKED = 1e30

KEYS1, KEYS0 = GROUPS * T, GROUPS * P
SCORES = KEYS1 + KEYS0
BLOCKS = SCORES // P

C_IDENT = 0
C_DIST = C_IDENT + P
C_BEFORE = C_DIST + SCORES
C_ONES = C_BEFORE + P
C_SLOT = C_ONES + P
C_PICK = C_SLOT + 2 * SLOTS
C_SLOPE = C_PICK + 3 * SLOTS
C_ALL = C_SLOPE + HEADS

V_MEM, V_MIX, V_CROSS = 0, DC, 2 * DC
V_BGATE = 3 * DC
V_CONV = V_BGATE + 2 * DC
V_ALL = V_CONV + CONV_K * DC


def constants():
    c = np.zeros((P, C_ALL), np.float32)
    c[:, C_IDENT:C_IDENT + P] = np.eye(P)
    q, k = np.arange(T)[:, None], np.arange(T)[None, :]
    for g, dil in enumerate(DILATION):
        d = q - k
        ok = (d >= 0) & (d % dil == 0) & (d <= WINDOW_STEPS * dil)
        dist = np.where(ok, d, MASKED).astype(np.float32)
        c[:, C_DIST + g * T:C_DIST + (g + 1) * T] = dist[P:, :]
        c[:, C_DIST + KEYS1 + g * P:C_DIST + KEYS1 + (g + 1) * P] = dist[:P, :P]
    c[:, C_BEFORE:C_BEFORE + P] = np.arange(P)[:, None] < np.arange(P)[None, :]
    c[:, C_ONES:C_ONES + P] = 1.0
    c[:, C_SLOT:C_SLOT + 2 * SLOTS] = np.tile(np.arange(SLOTS), 2)[None, :]
    for r in range(3):
        c[r, C_PICK + r * SLOTS:C_PICK + (r + 1) * SLOTS] = 1.0
    c[:, C_SLOPE:C_SLOPE + HEADS] = -(2.0 ** -np.arange(1.0, HEADS + 1)) * HD ** 0.5
    return c


def build(nc, io):
    ctx = ExitStack()
    with ctx:
        def sb(name, shape, dt=F32):
            return ctx.enter_context(nc.sbuf_tensor(name, shape, dt))

        def sem(name):
            return ctx.enter_context(nc.semaphore(name))

        SLOT_N = DC * 512
        ring = sb("ring", [P, 6 * SLOT_N])

        def slot(s):
            return ring[:, s * SLOT_N:(s + 1) * SLOT_N]

        const = sb("const", [P, C_ALL])
        ident = const[:, C_IDENT:C_IDENT + P]
        h = sb("h", [P, TT, D])
        xT = sb("xT", [P, DC, T])
        ycT = sb("ycT", [P, DC, T])
        memT = ycT
        qk = sb("qk", [P, 2, GROUPS, PAIRS, T])
        v = sb("v", [P, GROUPS, TT, AW])
        gates = sb("gates", [P, 2, DC, T])
        kmT = sb("kmT", [P, MH, T])
        vm = sb("vm", [P, TT, MH * MHD])
        prob = sb("prob", [P, SCORES])
        probT = sb("probT", [P, BLOCKS, P])
        ya = sb("ya", [P, TT, AW])
        vecs = sb("vecs", [P, V_ALL])
        small = sb("small", [P, 64])
        wr = sb("wr", [P, DC, E])
        rb = sb("rb", [P, E])
        g_moe = sb("g_moe", [P, DC])
        rounds_i = sb("rounds_i", [P, 1], I32)

        mem_in = v[:, :, :, :].rearrange("p g a n -> p (g a n)")[:, 0:TT * D].rearrange("p (a d) -> p a d", a=TT)
        normed = qk[:, 1, :, :, :].rearrange("p g a t -> p (g a t)")[:, 0:TT * D].rearrange("p (a d) -> p a d", a=TT)
        vec_rows = prob[0:V_ALL, 0:P]
        piece = [ring[:, 3 * SLOT_N + n * DC * 256:3 * SLOT_N + (n + 1) * DC * 256]
                 .rearrange("p (c n) -> p c n", c=DC) for n in range(5)]
        spare = ring[:, 3 * SLOT_N + 5 * DC * 256:6 * SLOT_N]
        stage_q = spare[:, 0:2 * GROUPS * T].rearrange("p (u g t) -> p u g t", u=2, g=GROUPS)
        gb_sb = spare[:, 2 * GROUPS * T:2 * GROUPS * T + 2 * T].rearrange("p (a t) -> p a t", a=2)
        gc_sb = sb("gc_sb", [P, 2, T])
        conv_z = sb("conv_z", [P, 2, T + CONV_K - 1])
        flat_q = qk[:, 0, :, :, :].rearrange("p g a t -> p (g a t)")
        mixT = flat_q[:, 0:DC * T].rearrange("p (c t) -> p c t", c=DC)
        yaT = flat_q[:, DC * T:DC * T + 4 * T].rearrange("p (j t) -> p j t", j=4)
        mix_a = gc_sb[:, :, :]
        mix_b = conv_z[:, :, 0:T]
        flat_v = v[:, :, :, :].rearrange("p g a n -> p (g a n)")
        qcT = flat_v[:, 0:MH * T].rearrange("p (m t) -> p m t", m=MH)
        ocT = flat_v[:, MH * T:2 * MH * T].rearrange("p (a m t) -> p a m t", a=TT, m=MH)
        flat_g = gates[:, :, :, :].rearrange("p a c t -> p (a c t)")
        pc = flat_g[:, 0:TT * MH * T].rearrange("p (a m k) -> p a m k", a=TT, m=MH)
        pcT = flat_g[:, TT * MH * T:2 * TT * MH * T].rearrange("p (a m b t) -> p a m b t", a=TT, m=MH, b=TT)

        logit = sb("logit", [P, TT, E + 4])
        top8 = sb("top8", [P, TT, 8])
        wanted = sb("wanted", [P, TT, 8])
        flat_pt = probT[:, :, :].rearrange("p b q -> p (b q)")
        logit_r = flat_pt[:, 0:TT * (E + 4)].rearrange("p (a e) -> p a e", a=TT)
        chosen = flat_pt[:, 128:128 + TT * E].rearrange("p (a e) -> p a e", a=TT)
        gate_w = flat_pt[:, 256:256 + TT * E].rearrange("p (a e) -> p a e", a=TT)
        place = sb("place", [P, TT, E + 2])
        f = 0

        def region(n):
            nonlocal f
            f += n
            assert f <= 2 * DC * T
            return flat_g[:, f - n:f]

        act_g = region(512)
        act_s = region(512)
        act_l = region(512)
        hdn = region(512)
        hdnT = region(512).rearrange("p (j s) -> p j s", j=4)
        y_sb = region(512)
        spread = region(2 * P).rearrange("p (a s) -> p a s", a=TT)
        spreadT = region(2 * P).rearrange("p (a t) -> p a t", a=TT)
        xg = prob[:, 0:DC * SLOTS].rearrange("p (c s) -> p c s", c=DC)
        pick = prob[:, DC * SLOTS:DC * SLOTS + TT * SLOTS].rearrange("p (a s) -> p a s", a=TT)
        bias = [ycT[:, 4 * u:4 * u + 4, :].rearrange("p c t -> p (c t)") for u in range(2)]
        b_down = kmT[0:E, :, :].rearrange("p m t -> p (m t)")
        gate_wT = vm[0:E, 0, 0:TT * P].rearrange("p (a t) -> p a t", a=TT)
        outp = qk[:, 0, :, :, :].rearrange("p g a t -> p (g a t)")[:, 0:TT * D].rearrange("p (a d) -> p a d", a=TT)
        g_fin = flat_v[:, 2 * MH * T:2 * MH * T + D]

        ps = ctx.enter_context(nc.psum_tensor("ps", [P, 8 * 512], F32))

        def bank(b, lo=0, n=512):
            return ps[:, b * 512 + lo:b * 512 + lo + n]

        sumsq, var, std, rstd = (small[:, 2 * k:2 * k + 2] for k in range(4))
        nmax = small[:, 8:12].rearrange("p (u a) -> p u a", u=2)
        psum_ = small[:, 12:16].rearrange("p (u a) -> p u a", u=2)
        rinv = small[:, 16:20].rearrange("p (u a) -> p u a", u=2)
        rowmax = small[:, 20:22]
        cmax, cneg, csum, cinv = (small[:, 22 + 8 * k:30 + 8 * k].rearrange("p (a m) -> p a m", a=TT)
                                  for k in range(4))
        topneg, topsum, topinv = (small[:, 54 + 2 * k:56 + 2 * k] for k in range(3))
        most = small[:, 60:61]
        rounds_f = small[:, 61:64]

        s_ident, s_const, s_vec, s_x, s_mem, s_wr, s_bd, s_gfin = (sem(n) for n in (
            "ident_loaded", "const_loaded", "vec_loaded", "x_loaded", "mem_loaded", "router_loaded", "down_bias_loaded", "final_gain_loaded"))
        s_ckv = [sem(f"ckv_loaded{n}") for n in range(2)]
        s_in = [sem(f"w_in_loaded{n}") for n in range(3)]
        s_piece = [sem(f"piece_loaded{n}") for n in range(5)]
        s_branch = sem("w_branch_loaded")
        s_wout = [sem(f"w_out_loaded{n}") for n in range(2)]
        s_cq, s_co = sem("w_cq_loaded"), sem("w_co_loaded")
        s_slot = [sem(f"expert_part_loaded{n}") for n in range(6)]
        s_bias = [sem(f"bias_loaded{n}") for n in range(2)]
        s_half = sem("first_half_used")
        s_zero = sem("zeros_written")
        s_dve = sem("vector_step")
        s_act = sem("scalar_step")
        s_vecT, s_vecs = sem("vec_turned"), sem("vec_ready")
        s_sq, s_var, s_std, s_nrm, s_trn, s_xT = (sem(n) for n in (
            "sumsq_ready", "var_ready", "std_ready", "normed_ready", "normed_turned", "xT_ready"))
        s_unit, s_evac = sem("projection_ready"), sem("projection_copied")
        s_stage, s_score, s_scread = sem("q_staged"), sem("scores_ready"), sem("scores_read")
        s_nmax, s_prob, s_ptp, s_pt = (sem(n) for n in (
            "max_ready", "prob_ready", "prob_turned", "probT_ready"))
        s_pv, s_ya = sem("attn_out_ready"), sem("ya_ready")
        s_xc, s_conv = sem("xc_used"), sem("conv_done")
        s_yat, s_yaT = sem("ya_turned"), sem("yaT_ready")
        s_mixp, s_mixread, s_mix = sem("branch_ready"), sem("branch_read"), sem("mix_ready")
        s_hp, s_h = sem("h_addend_ready"), sem("h_ready")
        s_cs, s_cm, s_ce, s_cn, s_ct, s_cpt, s_cv, s_co_t = (sem(n) for n in (
            "cross_scores", "cross_max", "cross_exp", "cross_prob", "cross_turned", "cross_probT",
            "cross_out", "cross_outT"))
        s_seed, s_w, s_wT = sem("sum_seeded"), sem("token_weights_ready"), sem("token_weights_turned")
        s_lg, s_top, s_ex, s_sel, s_pos, s_route = (sem(n) for n in (
            "logits_ready", "top_ready", "top_exp_ready", "chosen_ready", "positions_ready", "routes_ready"))
        s_rounds = sem("rounds_ready")
        s_pick, s_gat, s_xg = sem("pick_ready"), sem("gathered"), sem("xg_ready")
        s_gate, s_g, s_sig, s_up, s_lin, s_hdn = (sem(n) for n in (
            "gate_ready", "gate_clamped", "sigmoid_ready", "up_ready", "up_clamped", "hdn_ready"))
        s_spr, s_sprt, s_sprT = sem("spread_ready"), sem("spread_turned"), sem("spreadT_ready")
        s_ht, s_hT, s_y, s_ysb, s_sum = (sem(n) for n in (
            "hdn_turned", "hdnT_ready", "y_ready", "y_copied", "sum_updated"))
        s_out = sem("out_ready")
        s_store = sem("out_stored")

        FREE = 1
        UNITS_A = 6 * GROUPS
        UNITS_B = UNITS_A + 5 * PAIRS
        UNITS_M = UNITS_B + 4
        COPIED_B = 2 + UNITS_A + 4 * PAIRS
        PART_SLOT = (1, 2, 3, 4, 5, 0)

        w_in = io["w_in"].rearrange("(c p) n -> p c n", p=P)
        w_gate = io["w_gate"].rearrange("(c p) n -> p c n", p=P)
        w_in_q = io["w_in"].rearrange("(c p) (q n) -> q p c n", p=P, n=256)
        w_gate_q = io["w_gate"].rearrange("(c p) (q n) -> q p c n", p=P, n=256)
        CONV0 = GROUPS * 3 * AW

        def cols(s, n=512):
            return slot(s)[:, 0:DC * n].rearrange("p (c n) -> p c n", c=DC)

        def rows(s):
            return slot(s).rearrange("p (c n) -> p c n", c=4)

        block = ctx.enter_context(nc.Block())

        def load_expert(sp, e, before=None):
            wg = io["w_exp_gate"][bass.ds(e, 1)].rearrange("e (p c) n -> p (e c) n", c=DC)
            wu = io["w_exp_up"][bass.ds(e, 1)].rearrange("e (p c) n -> p (e c) n", c=DC)
            wd = io["w_exp_down"][bass.ds(e, 1)].rearrange("e (b p j) n -> p b (e j) n", b=2, j=4)
            parts = [wg[:, 0:4, :], wg[:, 4:8, :], wu[:, 0:4, :], wu[:, 4:8, :], wd[:, 0, :, :], wd[:, 1, :, :]]
            if before is None:
                free = ((s_unit, UNITS_B + 2), (s_unit, UNITS_M), (s_hp, 2), (s_hp, 4), (s_unit, UNITS_M + 2), (s_hp, 4 + 2 * TT))
            else:
                free = ((s_half, 3 * before - 2), (s_gate, before), (s_half, 3 * before - 1), (s_up, before),
                        (s_half, 3 * before), (s_y, before))
            for k in range(6):
                sp.wait_ge(*free[k])
                sp.dma_start(rows(PART_SLOT[k]), parts[k]).then_inc(s_slot[k], 16)

        @block.sync
        def _(sp):
            sp.dma_start(h[:, :, :], io["x"].rearrange("(a p) d -> p a d", p=P)).then_inc(s_x, 16)
            for n in range(3):
                sp.dma_start(cols(n), w_in[:, :, n * AW:(n + 1) * AW]).then_inc(s_in[n], 16)
            sp.dma_start(const[:, P:], io["const"][:, P:]).then_inc(s_const, 16)

            def load_pieces(i, units):
                for n in range(5):
                    src = w_in_q[bass.ds(CONV0 // 256 + 4 * n + i, 1)] if n < 3 else \
                        w_gate_q[bass.ds(4 * (n - 3) + i, 1)]
                    if units:
                        sp.wait_ge(s_unit, units(n))
                    sp.dma_start(piece[n], src.rearrange("q p c n -> p (q c) n")).then_inc(s_piece[n], 16)
            load_pieces(0, None)
            with sp.Fori(1, GROUPS) as g:
                for n in range(3):
                    sp.wait_ge(s_unit, 6 * g - 4 + 2 * n)
                    sp.dma_start(cols(n), w_in[:, :, bass.ds(3 * AW * g + n * AW, AW)]).then_inc(s_in[n], 16)
            sp.wait_ge(s_unit, UNITS_A)
            sp.dma_start(rows(0), io["w_branch_attn"].rearrange("(c p) n -> p c n", p=P)).then_inc(s_branch, 16)
            for n in range(2):
                sp.dma_start(rows(1 + n), io["w_branch_conv"].rearrange("(b c p) n -> b p c n", b=2, p=P)[n])\
                    .then_inc(s_branch, 16)
            with sp.Fori(0, PAIRS - 1) as i:
                load_pieces(i + 1, lambda n: UNITS_A + 5 * i + 1 + n)
            sp.wait_ge(s_unit, UNITS_B)
            sp.dma_start(mem_in, io["mem"].rearrange("(a p) d -> p a d", p=P)).then_inc(s_mem, 16)
            for n in range(2):
                sp.dma_start(cols(3 + n), io["w_out"].rearrange("(c p) n -> p c n", p=P)[:, :, n * 512:(n + 1) * 512])\
                    .then_inc(s_wout[n], 16)
            sp.wait_ge(s_conv, FREE + PAIRS)
            sp.dma_start(cols(5), io["w_cq"].rearrange("(c p) n -> p c n", p=P)).then_inc(s_cq, 16)
            sp.wait_ge(s_mixp, DC)
            for n in range(2):
                sp.dma_start(cols(1 + n), io["w_ckv"].rearrange("(c p) n -> p c n", p=P)[:, :, n * 512:(n + 1) * 512])\
                    .then_inc(s_ckv[n], 16)
            sp.dma_start(rows(0), io["w_co"].rearrange("(c p) n -> p c n", p=P)).then_inc(s_co, 16)
            load_expert(sp, 0)
            with sp.Fori(1, E) as e:
                load_expert(sp, e, e)
            sp.wait_ge(s_rounds, 1)
            rounds = sp.value_load(rounds_i[0:1, 0:1], min_val=1, max_val=T // SLOTS)
            with sp.If(rounds > 1):
                with sp.Fori(1, rounds) as r:
                    with sp.Fori(0, E) as e:
                        load_expert(sp, e, E * r + e)
            for tt in range(TT):
                sp.wait_ge(s_out, tt + 1)
                sp.dma_start(io["out"][tt * P:(tt + 1) * P, :], outp[:, tt, :]).then_inc(s_store, 16)
            sp.wait_ge(s_store, 16 * TT)

        @block.gpsimd
        def _(pool):
            nc.gpsimd.memset(stage_q, 0.0).then_inc(s_zero, 1)
            nc.gpsimd.memset(conv_z[:, :, 0:CONV_K - 1], 0.0).then_inc(s_zero, 1)
            nc.gpsimd.memset(logit[:, :, E:E + 4], SENTINEL).then_inc(s_zero, 1)
            nc.gpsimd.memset(wanted[:, :, 4:8], SENTINEL).then_inc(s_zero, 1)
            nc.gpsimd.memset(place[:, :, E:E + 2], -1.0).then_inc(s_zero, 1)
            pool.wait_ge(s_zero, 5)
            pool.wait_ge(s_evac, 2 + UNITS_A)
            with pool.Fori(0, PAIRS) as i:
                for u in range(2):
                    rs = slice(u * HD, (u + 1) * HD)
                    pool.wait_ge(s_score, 2 * i + u + 1)
                    nc.gpsimd.tensor_copy(stage_q[rs, u, :, :], qk[rs, 0, :, bass.ds(i, 1), :]).then_inc(s_stage, 1)
                    pool.wait_ge(s_stage, 2 * i + u + 1)
            pool.wait_ge(s_unit, UNITS_M)
            for u in range(2):
                nc.gpsimd.memset(bias[u], 0.0).then_inc(s_zero, 1)
            pool.wait_ge(s_zero, 7)

            def load_bias(u, e):
                for k, name in enumerate(("b_exp_gate", "b_exp_up")):
                    pool.dma_start(bias[u][k:k + 1, :], io[name][bass.ds(e, 1), :]).then_inc(s_bias[u], 16)

            for u in range(2):
                load_bias(u, u)
            with pool.Fori(1, E // 2) as i:
                for u in range(2):
                    pool.wait_ge(s_up, 2 * i + u - 1)
                    load_bias(u, 2 * i + u)
            pool.wait_ge(s_rounds, 1)
            rounds = pool.value_load(rounds_i[0:1, 0:1], min_val=1, max_val=T // SLOTS)
            with pool.If(rounds > 1):
                with pool.Fori(1, rounds) as r:
                    with pool.Fori(0, E // 2) as i:
                        for u in range(2):
                            pool.wait_ge(s_up, E * r + 2 * i + u - 1)
                            load_bias(u, 2 * i + u)

        @block.tensor
        def _(pe):
            def turn_vectors():
                pe.wait_ge(s_ident, 16)
                pe.wait_ge(s_vec, 16 * 5)
                nc.tensor.transpose(bank(2, 0, V_ALL), vec_rows, ident[0:V_ALL, 0:V_ALL]).then_inc(s_vecT, 1)

            def turn_normed(k):
                for tt in range(TT):
                    pe.wait_ge(s_nrm, TT * k + tt + 1)
                    for c in range(DC):
                        last = nc.tensor.transpose(bank(4 + 2 * tt, c * P, P), normed[:, tt, c * P:(c + 1) * P], ident)
                    last.then_inc(s_trn, 1)

            def project_T(b, w, c0, src):
                for j in range(2):
                    for c in range(DC):
                        last = nc.tensor.matmul(bank(b, j * T, T), w[:, c, c0 + j * P:c0 + (j + 1) * P], src[:, c, :],
                                                start=(c == 0), stop=(c == DC - 1))
                return last

            def project(b, w, tt, src):
                for c in range(DC):
                    last = nc.tensor.matmul(bank(b), src[:, c, tt * P:(tt + 1) * P], w[:, c, :],
                                            start=(c == 0), stop=(c == DC - 1))
                return last

            pe.nop().then_inc(s_score, 2)
            pe.nop().then_inc(s_sprt, FREE)
            turn_vectors()
            turn_normed(0)
            pe.wait_ge(s_xT, TT)
            with pe.Fori(0, GROUPS) as g:
                for n in range(3):
                    pe.wait_ge(s_in[n], 16 * g + 16)
                    for j in range(2):
                        pe.wait_ge(s_evac, 6 * g + 2 * n + j + 1)
                        if n < 2:
                            last = project_T(j, cols(n), j * 256, xT)
                        else:
                            last = project(j, cols(n), j, xT)
                        last.then_inc(s_unit, 1)

            def scores(i, u):
                pe.wait_ge(s_stage, 2 * i + u + 1)
                pe.wait_ge(s_scread, FREE + 2 * i + u)
                for g in range(GROUPS):
                    nc.tensor.matmul(ps[:, 2 * 512 + g * T:2 * 512 + (g + 1) * T], stage_q[:, u, g, P:T],
                                     qk[:, 1, g, bass.ds(i, 1), :], start=True, stop=True)
                for g in range(GROUPS):
                    last = nc.tensor.matmul(bank(4, g * P, P), stage_q[:, u, g, 0:P],
                                            qk[:, 1, g, bass.ds(i, 1), 0:P], start=True, stop=True)
                last.then_inc(s_score, 1)

            def turn_probs(i, u):
                pe.wait_ge(s_prob, 2 * (2 * i + u) + 2)
                pe.wait_ge(s_ya, FREE + 2 * i + u)
                for b in range(BLOCKS):
                    last = nc.tensor.transpose(bank(5, b * P, P), prob[:, b * P:(b + 1) * P], ident)
                last.then_inc(s_ptp, 1)

            def attend(i, u):
                pe.wait_ge(s_pt, 2 * i + u + 1)
                for tt, (b0, kts) in enumerate(((2 * GROUPS, 1), (0, 2))):
                    for g in range(GROUPS):
                        for kt in range(kts):
                            last = nc.tensor.matmul(
                                bank(7, 256 + tt * HD, HD), probT[:, b0 + g * kts + kt, :],
                                v[:, g, kt, bass.ds(2 * HD * i + u * HD, HD)],
                                start=(g == 0 and kt == 0), stop=(g == GROUPS - 1 and kt == kts - 1))
                last.then_inc(s_pv, 1)

            def unit(i, n):
                pe.wait_ge(s_piece[n], 16 * i + 16)
                if n in (0, 2, 3):
                    pe.wait_ge(s_evac, 2 + UNITS_A + 4 * i + {0: 0, 2: 1, 3: 2}[n])
                if n == 4:
                    pe.wait_ge(s_xc, i + 1)
                project_T(n % 2, piece[n], 0, xT).then_inc(s_unit, 1)

            with pe.Fori(0, PAIRS) as i:
                scores(i, 0)
                unit(i, 0)
                turn_probs(i, 0)
                scores(i, 1)
                unit(i, 1)
                attend(i, 0)
                unit(i, 2)
                turn_probs(i, 1)
                unit(i, 3)
                attend(i, 1)
                unit(i, 4)

            pe.wait_ge(s_ya, FREE + HEADS)
            for j in range(4):
                for tt in range(TT):
                    last = nc.tensor.transpose(bank(2, j * T + tt * P, P), ya[:, tt, j * P:(j + 1) * P], ident)
            last.then_inc(s_yat, 1)
            pe.wait_ge(s_branch, 16 * 3)
            pe.wait_ge(s_yaT, 1)
            pe.wait_ge(s_conv, FREE + PAIRS)
            pe.wait_ge(s_evac, COPIED_B)
            for m in range(DC):
                if m >= 2:
                    pe.wait_ge(s_mixread, m - 1)
                for c in range(4):
                    nc.tensor.matmul(bank(m % 2, 0, T), rows(0)[:, c, m * P:(m + 1) * P], yaT[:, c, :],
                                     start=(c == 0), stop=(c == 3))
                for c in range(DC):
                    last = nc.tensor.matmul(bank(m % 2, T, T), rows(1 + c // 4)[:, c % 4, m * P:(m + 1) * P],
                                            ycT[:, c, :], start=(c == 0), stop=(c == DC - 1))
                last.then_inc(s_mixp, 1)
            turn_normed(1)
            pe.wait_ge(s_mix, DC)
            for half in range(2):
                pe.wait_ge(s_wout[half], 16)
                if half:
                    pe.wait_ge(s_xT, 2 * TT)
                for tt in range(TT):
                    project(2 + 2 * half + tt, cols(3 + half), tt, mixT).then_inc(s_hp, 1)
            pe.wait_ge(s_ckv[0], 16)
            pe.wait_ge(s_xT, 2 * TT)
            pe.wait_ge(s_mixread, DC)
            for j in range(2):
                project_T(j, cols(1), j * 256, memT).then_inc(s_unit, 1)
            pe.wait_ge(s_ckv[1], 16)
            for tt in range(TT):
                pe.wait_ge(s_evac, COPIED_B + tt + 1)
                project(tt, cols(2), tt, memT).then_inc(s_unit, 1)

            turn_normed(2)
            pe.wait_ge(s_cq, 16)
            pe.wait_ge(s_xT, 3 * TT)
            for j in range(2):
                pe.wait_ge(s_evac, COPIED_B + 3 + j)
                project_T(j, cols(5), j * 256, xT).then_inc(s_unit, 1)
            pe.wait_ge(s_evac, COPIED_B + 6)
            for tt in range(TT):
                for m in range(MH):
                    last = nc.tensor.matmul(bank(2 + 2 * tt, m * T, T), qcT[:, m, tt * P:(tt + 1) * P], kmT[:, m, :],
                                            start=True, stop=True)
                last.then_inc(s_cs, 1)
            for tt in range(TT):
                pe.wait_ge(s_cn, tt + 1)
                for m in range(MH):
                    for b in range(TT):
                        last = nc.tensor.transpose(bank((6, 2)[tt], (m * TT + b) * P, P),
                                                   pc[:, tt, m, b * P:(b + 1) * P], ident)
                last.then_inc(s_ct, 1)
                pe.wait_ge(s_cpt, tt + 1)
                for m in range(MH):
                    for b in range(TT):
                        last = nc.tensor.matmul(bank(tt, m * P, P), vm[:, b, m * MHD:(m + 1) * MHD],
                                                pcT[:, tt, m, b, :], start=(b == 0), stop=(b == TT - 1))
                last.then_inc(s_cv, 1)
            pe.wait_ge(s_co, 16)
            for tt in range(TT):
                pe.wait_ge(s_co_t, tt + 1)
                for half in range(2):
                    for m in range(MH):
                        last = nc.tensor.matmul(bank(4 + 2 * tt + half), ocT[:, tt, m, :],
                                                rows(0)[:, m, half * 512:(half + 1) * 512],
                                                start=(m == 0), stop=(m == MH - 1))
                    last.then_inc(s_hp, 1)

            pe.wait_ge(s_h, 2 * 2 * TT)
            for tt in range(TT):
                for half in range(2):
                    last = nc.tensor.matmul(bank(2 * tt + half), ident, h[:, tt, half * 512:(half + 1) * 512],
                                            start=True, stop=False, skip_group_check=True)
            turn_normed(3)
            pe.wait_ge(s_xT, 4 * TT)
            pe.wait_ge(s_wr, 48)
            for tt in range(TT):
                for c in range(DC):
                    last = nc.tensor.matmul(bank(6, tt * E, E), xT[:, c, tt * P:(tt + 1) * P], wr[:, c, :],
                                            start=(c == 0), stop=(c == DC - 1))
            last.then_inc(s_lg, 1)
            pe.wait_ge(s_sel, TT)
            before, ones = const[:, C_BEFORE:C_BEFORE + P], const[:, C_ONES:C_ONES + P]
            nc.tensor.matmul(bank(7, 0, E), before, chosen[:, 0, :], start=True, stop=True)
            nc.tensor.matmul(bank(7, E, E), ones, chosen[:, 0, :], start=True, stop=False)
            nc.tensor.matmul(bank(7, E, E), before, chosen[:, 1, :], start=False, stop=True)
            nc.tensor.matmul(bank(7, 2 * E, E), ones, chosen[:, 0, :], start=True, stop=False)
            nc.tensor.matmul(bank(7, 2 * E, E), ones, chosen[:, 1, :], start=False, stop=True).then_inc(s_pos, 1)

            def gather(count):
                pe.wait_ge(s_pick, 2 * count)
                for c in range(DC):
                    for tt in range(TT):
                        last = nc.tensor.matmul(bank(6, c * SLOTS, SLOTS), normed[:, tt, c * P:(c + 1) * P],
                                                pick[:, tt, :], start=(tt == 0), stop=(tt == TT - 1))
                last.then_inc(s_gat, 1)

            def wide(b, k0, u, w0, row, count):
                for half in range(2 if row is not None else 0):
                    nc.tensor.matmul(bank(b)[half * SLOTS:(half + 1) * SLOTS, :],
                                     const[:, C_PICK + row * SLOTS:C_PICK + (row + 1) * SLOTS],
                                     bias[u][:, half * 512:(half + 1) * 512], start=True, stop=False)
                for part in range(2):
                    pe.wait_ge(s_slot[k0 + part], 16 * count)
                    for j in range(4):
                        for half in range(2):
                            last = nc.tensor.matmul(bank(b)[half * SLOTS:(half + 1) * SLOTS, :],
                                                    w0(part, j), rows(PART_SLOT[k0 + part])[:, j, half * 512:(half + 1) * 512],
                                                    start=(row is None and part == 0 and j == 0),
                                                    stop=(part == 1 and j == 3))
                    if part == 0:
                        last.then_inc(s_half, 1)
                return last

            def expert_body(u, count, pairs, gathers):
                pe.wait_ge(s_xg, gathers)
                pe.wait_ge(s_bias[u], 32 * pairs)
                wide(4, 0, u, lambda part, j: xg[:, 4 * part + j, :], 0, count).then_inc(s_gate, 1)
                wide(5, 2, u, lambda part, j: xg[:, 4 * part + j, :], 1, count).then_inc(s_up, 1)
                pe.wait_ge(s_spr, 2 * count)
                for tt in range(TT):
                    last = nc.tensor.transpose(bank(7, tt * P, P), spread[:, tt, :], ident)
                last.then_inc(s_sprt, 1)
                gather(gathers + 1)
                pe.wait_ge(s_hdn, count)
                pe.wait_ge(s_xg, gathers + 1)
                for j in range(4):
                    last = nc.tensor.transpose(bank(6, j * P, P),
                                               hdn.rearrange("p (n j) -> p j n", j=4)[:, j, :], ident)
                last.then_inc(s_ht, 1)
                pe.wait_ge(s_hT, count)
                pe.wait_ge(s_sprT, count)
                wide(7, 4, u, lambda part, j: hdnT[:, j, part * SLOTS:(part + 1) * SLOTS], None, count).then_inc(s_y, 1)
                pe.wait_ge(s_ysb, count)
                for tt in range(TT):
                    for half in range(2):
                        rs = slice(half * SLOTS, (half + 1) * SLOTS)
                        last = nc.tensor.matmul(bank(2 * tt + half), spreadT[rs, tt, :], y_sb[rs, :],
                                                start=False, stop=False, skip_group_check=True)
                last.then_inc(s_sum, 1)

            gather(1)
            pe.wait_ge(s_bd, 16)
            pe.wait_ge(s_w, 1)
            for tt in range(TT):
                last = nc.tensor.transpose(bank(7, 128 + tt * P, P)[0:E, :], gate_w[:, tt, :], ident)
            last.then_inc(s_seed, 1)
            pe.wait_ge(s_wT, 1)
            for tt in range(TT):
                for half in range(2):
                    last = nc.tensor.matmul(bank(2 * tt + half), gate_wT[:, tt, :],
                                            b_down[:, half * 512:(half + 1) * 512],
                                            start=False, stop=False, skip_group_check=True)
            last.then_inc(s_seed, 1)
            with pe.Fori(0, E // 2) as i:
                for u in range(2):
                    expert_body(u, 2 * i + u + 1, i + 1, 2 * i + u + 1)
            pe.wait_ge(s_rounds, 1)
            rounds = pe.value_load(rounds_i[0:1, 0:1], min_val=1, max_val=T // SLOTS)
            with pe.If(rounds > 1):
                with pe.Fori(1, rounds) as r:
                    gather((E + 1) * r + 1)
                    with pe.Fori(0, E // 2) as i:
                        for u in range(2):
                            expert_body(u, E * r + 2 * i + u + 1, E // 2 * r + i + 1, (E + 1) * r + 2 * i + u + 1)

        @block.scalar
        def _(act):
            act.nop().then_inc(s_evac, 2)
            act.dma_start(ident, io["const"][:, 0:P]).then_inc(s_ident, 16)
            for row, name, n in ((V_MEM, "norm_mem", DC), (V_MIX, "norm_mix", DC), (V_CROSS, "norm_cross", DC),
                                 (V_BGATE, "b_gate", 2 * DC), (V_CONV, "conv_w", CONV_K * DC)):
                act.dma_start(vec_rows[row:row + n, :], io[name].rearrange("(a n) -> a n", n=P)).then_inc(s_vec, 16)
            act.dma_start(wr[:, :, :], io["router_w"].rearrange("(p c) e -> p c e", c=DC)).then_inc(s_wr, 16)
            act.dma_start(rb[:, :], io["router_b"].rearrange("(a e) -> a e", a=1).to_broadcast([P, E])).then_inc(s_wr, 16)
            act.dma_start(g_moe[:, :], io["norm_moe"].rearrange("(p c) -> p c", c=DC)).then_inc(s_wr, 16)

            def sumsq_std(k, src):
                for tt in range(TT):
                    nc.scalar.activation(normed[:, tt, :], src(tt), ACT.Square,
                                         accum_out=sumsq[:, tt:tt + 1]).then_inc(s_sq, 1)
                act.wait_ge(s_var, k + 1)
                nc.scalar.activation(std, var, ACT.Sqrt).then_inc(s_std, 1)

            def copy_unit(n, dst, src):
                act.wait_ge(s_unit, n)
                nc.scalar.copy(dst, src).then_inc(s_evac, 1)

            two = "p (a t) -> p a t"
            act.wait_ge(s_x, 16)
            sumsq_std(0, lambda tt: h[:, tt, :])
            act.wait_ge(s_trn, TT)
            with act.Fori(0, GROUPS) as g:
                for n in range(3):
                    for j in range(2):
                        if n < 2:
                            dst = qk[:, n, bass.ds(g, 1), 2 * j:2 * j + 2, :]
                            src = bank(j).rearrange("p (g a t) -> p g a t", g=1, a=2)
                        else:
                            dst, src = v[:, bass.ds(g, 1), j, :], bank(j).rearrange("p (g n) -> p g n", g=1)
                        copy_unit(6 * g + 2 * n + j + 1, dst, src)
            def exps(i, u):
                act.wait_ge(s_nmax, 2 * i + u + 1)
                for tt, cs in ((0, slice(KEYS1, SCORES)), (1, slice(0, KEYS1))):
                    nc.scalar.activation(prob[:, cs], prob[:, cs], ACT.Exp, bias=nmax[:, u, tt:tt + 1],
                                         scale=HD ** -0.5, accum_out=psum_[:, u, tt:tt + 1]).then_inc(s_prob, 1)

            def copy_probs(i, u):
                act.wait_ge(s_ptp, 2 * i + u + 1)
                nc.scalar.copy(probT[:, :, :], ps[:, 5 * 512:5 * 512 + SCORES].rearrange("p (b q) -> p b q", q=P))\
                    .then_inc(s_pt, 1)

            with act.Fori(0, PAIRS) as i:
                exps(i, 0)
                act.wait_ge(s_conv, FREE + i)
                copy_unit(UNITS_A + 5 * i + 1, gb_sb, bank(0).rearrange(two, a=2))
                copy_probs(i, 0)
                exps(i, 1)
                copy_unit(UNITS_A + 5 * i + 2, gc_sb[:, :, :], bank(1).rearrange(two, a=2))
                copy_probs(i, 1)
                for b in range(2):
                    act.wait_ge(s_unit, UNITS_A + 5 * i + 4 + b)
                    for j in range(2):
                        ins = nc.scalar.activation(gates[:, b, bass.ds(2 * i + j, 1), :],
                                                   bank(1 - b, j * T, T).rearrange("p (a t) -> p a t", a=1),
                                                   ACT.Sigmoid, bias=vecs[:, bass.ds(V_BGATE + b * DC + j + 2 * i, 1)])
                    ins.then_inc(s_evac, 1)
            act.wait_ge(s_yat, 1)
            nc.scalar.copy(yaT, ps[:, 2 * 512:4 * 512].rearrange("p (j t) -> p j t", j=4)).then_inc(s_yaT, 1)
            act.wait_ge(s_mem, 16)
            sumsq_std(1, lambda tt: mem_in[:, tt, :])
            act.wait_ge(s_h, 2 * TT)
            act.wait_ge(s_trn, 2 * TT)
            sumsq_std(2, lambda tt: h[:, tt, :])
            for j in range(2):
                copy_unit(UNITS_B + 1 + j, kmT[:, 2 * j:2 * j + 2, :], bank(j).rearrange(two, a=2))
            for tt in range(TT):
                copy_unit(UNITS_B + 3 + tt, vm[:, tt, :], bank(tt))
            for j in range(2):
                copy_unit(UNITS_M + 1 + j, qcT[:, 2 * j:2 * j + 2, :], bank(j).rearrange(two, a=2))
            for tt in range(TT):
                act.wait_ge(s_cm, tt + 1)
                for m in range(MH):
                    nc.scalar.activation(pc[:, tt, m, :], bank(2 + 2 * tt, m * T, T), ACT.Exp,
                                         bias=cneg[:, tt, m:m + 1], scale=MHD ** -0.5,
                                         accum_out=csum[:, tt, m:m + 1]).then_inc(s_ce, 1)
            for tt in range(TT):
                act.wait_ge(s_ct, tt + 1)
                nc.scalar.copy(pcT[:, tt, :, :, :], bank((6, 2)[tt], 0, 1024)
                               .rearrange("p (m b t) -> p m b t", m=MH, b=TT)).then_inc(s_cpt, 1)
                act.wait_ge(s_cv, tt + 1)
                nc.scalar.copy(ocT[:, tt, :, :], bank(tt).rearrange("p (m t) -> p m t", m=MH)).then_inc(s_co_t, 1)
            act.wait_ge(s_h, 4 * TT)
            sumsq_std(3, lambda tt: h[:, tt, :])
            act.dma_start(g_fin, io["norm_final"].rearrange("(a d) -> a d", a=1).to_broadcast([P, D])).then_inc(s_gfin, 16)
            act.dma_start(b_down, io["b_exp_down"]).then_inc(s_bd, 16)
            act.wait_ge(s_top, 1)
            for tt in range(TT):
                nc.scalar.activation(gate_w[:, tt, :], logit[:, tt, 0:E], ACT.Exp,
                                     bias=topneg[:, tt:tt + 1]).then_inc(s_ex, 1)
            act.wait_ge(s_seed, 1)
            nc.scalar.copy(gate_wT, bank(7, 128, TT * P)[0:E, :].rearrange("p (a t) -> p a t", a=TT)).then_inc(s_wT, 1)

            def expert_body(count):
                act.wait_ge(s_g, count)
                nc.scalar.activation(act_s, act_g, ACT.Sigmoid, scale=ALPHA).then_inc(s_sig, 1)
                act.wait_ge(s_sprt, FREE + count)
                nc.scalar.copy(spreadT, bank(7, 0, TT * P).rearrange("p (a t) -> p a t", a=TT)).then_inc(s_sprT, 1)
                act.wait_ge(s_ht, count)
                nc.scalar.copy(hdnT, bank(6).rearrange("p (j s) -> p j s", j=4)).then_inc(s_hT, 1)
                act.wait_ge(s_y, count)
                nc.scalar.copy(y_sb, bank(7)).then_inc(s_ysb, 1)

            with act.Fori(0, E // 2) as i:
                for u in range(2):
                    expert_body(2 * i + u + 1)
            act.wait_ge(s_sum, E)
            act.wait_ge(s_rounds, 1)
            rounds = act.value_load(rounds_i[0:1, 0:1], min_val=1, max_val=T // SLOTS)
            with act.If(rounds > 1):
                with act.Fori(1, rounds) as r:
                    with act.Fori(0, E // 2) as i:
                        for u in range(2):
                            expert_body(E * r + 2 * i + u + 1)
                    act.wait_ge(s_sum, E * r + E)
            sumsq_std(4, lambda tt: bank(2 * tt, 0, D))

        @block.vector
        def _(dve):
            steps = [0]

            def link(ins):
                steps[0] += 1
                ins.then_inc(s_dve, 1)
                dve.wait_ge(s_dve, steps[0])

            def norm(k, src, permuted=False):
                dve.wait_ge(s_sq, TT * (k + 1))
                nc.vector.tensor_scalar(var, sumsq, 1.0 / D, EPS, ALU.mult, ALU.add).then_inc(s_var, 1)
                dve.wait_ge(s_std, k + 1)
                link(nc.vector.reciprocal(rstd, std))
                for tt in range(TT):
                    dst, x = normed[:, tt, :], src(tt)
                    if permuted:
                        dst = dst.rearrange("t (c p) -> t c p", c=DC)
                        x = x.rearrange("t (p c) -> t c p", c=DC)
                    nc.vector.tensor_scalar(dst, x, rstd[:, tt:tt + 1], None, ALU.mult).then_inc(s_nrm, 1)

            def gained(k, dst, gain):
                for tt in range(TT):
                    dve.wait_ge(s_trn, TT * k + tt + 1)
                    nc.vector.tensor_tensor(dst[:, :, tt * P:(tt + 1) * P],
                                            bank(4 + 2 * tt, 0, D).rearrange("p (c t) -> p c t", c=DC),
                                            gain.rearrange("p (c o) -> p c o", o=1).to_broadcast([P, DC, P]),
                                            ALU.mult).then_inc(s_xT, 1)

            dve.nop().then_inc(s_scread, FREE)
            dve.nop().then_inc(s_ya, FREE)
            dve.nop().then_inc(s_conv, FREE)
            dve.wait_ge(s_vecT, 1)
            link(nc.vector.tensor_copy(vecs[:, :], bank(2, 0, V_ALL)))
            norm(0, lambda tt: h[:, tt, :])
            gained(0, xT, vecs[:, V_MIX:V_MIX + DC])

            def soft(i, u, n):
                dve.wait_ge(s_score, 2 + 2 * i + u + 1)
                slope = const[:, bass.ds(C_SLOPE + u + 2 * i, 1)]
                for cs, b in ((slice(0, KEYS1), 2), (slice(KEYS1, SCORES), 4)):
                    ins = nc.vector.scalar_tensor_tensor(
                        out=prob[:, cs], in0=const[:, C_DIST + cs.start:C_DIST + cs.stop], scalar=slope,
                        in1=bank(b, 0, cs.stop - cs.start), op0=ALU.mult, op1=ALU.add)
                ins.then_inc(s_scread, 1)
                dve.wait_ge(s_scread, FREE + 2 * i + u + 1)
                for tt, cs in ((0, slice(KEYS1, SCORES)), (1, slice(0, KEYS1))):
                    ins = nc.vector.tensor_reduce(rowmax[:, tt:tt + 1], prob[:, cs], AX_X, ALU.max)
                n(ins)
                nc.vector.tensor_scalar(nmax[:, u, :], rowmax, -HD ** -0.5, None, ALU.mult).then_inc(s_nmax, 1)

            def take_out(i, u, n):
                dve.wait_ge(s_prob, 2 * (2 * i + u) + 2)
                n(nc.vector.reciprocal(rinv[:, u, :], psum_[:, u, :]))
                dve.wait_ge(s_pv, 2 * i + u + 1)
                for tt in range(TT):
                    ins = nc.vector.tensor_scalar(ya[:, tt, bass.ds(2 * HD * i + u * HD, HD)],
                                                  bank(7, 256 + tt * HD, HD), rinv[:, u, tt:tt + 1], None, ALU.mult)
                ins.then_inc(s_ya, 1)

            dve.wait_ge(s_const, 16)
            dve.wait_ge(s_zero, 5)
            base, per = steps[0], 7
            with dve.Fori(0, PAIRS) as i:
                k = [0]

                def n(ins):
                    k[0] += 1
                    ins.then_inc(s_dve, 1)
                    dve.wait_ge(s_dve, base + per * i + k[0])

                soft(i, 0, n)
                soft(i, 1, n)
                take_out(i, 0, n)
                dve.wait_ge(s_unit, UNITS_A + 5 * i + 3)
                dve.wait_ge(s_evac, 2 + UNITS_A + 4 * i + 2)
                nc.vector.tensor_tensor(conv_z[:, :, CONV_K - 1:], bank(0).rearrange("p (a t) -> p a t", a=2),
                                        gc_sb[:, :, :], ALU.mult).then_inc(s_xc, 1)
                dve.wait_ge(s_xc, i + 1)
                for tap in range(CONV_K):
                    for j in range(2):
                        w = vecs[:, bass.ds(V_CONV + tap * DC + j + 2 * i, 1)]
                        z = conv_z[:, j:j + 1, tap:tap + T]
                        y = ycT[:, bass.ds(2 * i + j, 1), :]
                        if tap == 0:
                            ins = nc.vector.tensor_scalar(y, z, w, None, ALU.mult)
                        else:
                            ins = nc.vector.scalar_tensor_tensor(out=y, in0=z, scalar=w,
                                                                 in1=y, op0=ALU.mult, op1=ALU.add)
                    n(ins)
                nc.vector.tensor_tensor(ycT[:, bass.ds(2 * i, 2), :], ycT[:, bass.ds(2 * i, 2), :], gb_sb, ALU.mult)\
                    .then_inc(s_conv, 1)
                take_out(i, 1, n)
            assert k[0] == per, k
            steps[0] += per * PAIRS

            for m in range(DC):
                dve.wait_ge(s_mixp, m + 1)
                nc.vector.tensor_tensor(mix_a[:, m % 2, :], bank(m % 2, 0, T), gates[:, 0, m, :], ALU.mult)
                nc.vector.tensor_tensor(mix_b[:, m % 2, :], bank(m % 2, T, T), gates[:, 1, m, :], ALU.mult)\
                    .then_inc(s_mixread, 1)
                dve.wait_ge(s_mixread, m + 1)
                nc.vector.tensor_tensor(mixT[:, m, :], mix_a[:, m % 2, :], mix_b[:, m % 2, :], ALU.add)\
                    .then_inc(s_mix, 1)
                if m == 3:
                    norm(1, lambda tt: mem_in[:, tt, :])
            gained(1, memT, vecs[:, V_MEM:V_MEM + DC])
            for half in range(2):
                for tt in range(TT):
                    dve.wait_ge(s_hp, 2 * half + tt + 1)
                    hh = h[:, tt, half * 512:(half + 1) * 512]
                    nc.vector.tensor_tensor(hh, bank(2 + 2 * half + tt), hh, ALU.add).then_inc(s_h, 1)
            dve.wait_ge(s_h, 2 * TT)
            norm(2, lambda tt: h[:, tt, :])
            gained(2, xT, vecs[:, V_CROSS:V_CROSS + DC])
            for tt in range(TT):
                dve.wait_ge(s_cs, tt + 1)
                link(nc.vector.tensor_reduce(cmax[:, tt, :], bank(2 + 2 * tt, 0, MH * T)
                                             .rearrange("p (m k) -> p m k", m=MH), AX_X, ALU.max))
                nc.vector.tensor_scalar(cneg[:, tt, :], cmax[:, tt, :], -MHD ** -0.5, None, ALU.mult).then_inc(s_cm, 1)
            for tt in range(TT):
                dve.wait_ge(s_ce, MH * (tt + 1))
                link(nc.vector.reciprocal(cinv[:, tt, :], csum[:, tt, :]))
                nc.vector.tensor_tensor(pc[:, tt, :, :], pc[:, tt, :, :],
                                        cinv[:, tt, :].rearrange("p (m o) -> p m o", o=1).to_broadcast([P, MH, T]),
                                        ALU.mult).then_inc(s_cn, 1)
            for tt in range(TT):
                for half in range(2):
                    dve.wait_ge(s_hp, 2 * TT + 2 * tt + half + 1)
                    hh = h[:, tt, half * 512:(half + 1) * 512]
                    nc.vector.tensor_tensor(hh, bank(4 + 2 * tt + half), hh, ALU.add).then_inc(s_h, 1)
            dve.wait_ge(s_h, 4 * TT)
            norm(3, lambda tt: h[:, tt, :], permuted=True)
            dve.wait_ge(s_wr, 48)
            gained(3, xT, g_moe[:, :])
            dve.wait_ge(s_lg, 1)
            for tt in range(TT):
                ins = nc.vector.tensor_tensor(logit[:, tt, 0:E], bank(6, tt * E, E), rb[:, :], ALU.add)
            link(ins)
            for tt in range(TT):
                ins = nc.vector.max(top8[:, tt, :], logit[:, tt, 0:E])
            link(ins)
            nc.vector.tensor_scalar(topneg, top8[:, :, 0], -1.0, None, ALU.mult).then_inc(s_top, 1)
            link(nc.vector.tensor_copy(wanted[:, :, 0:TOPK], top8[:, :, 0:TOPK]))
            for tt in range(TT):
                ins = nc.vector.match_replace(out=logit_r[:, tt, :], in_to_replace=wanted[:, tt, :],
                                              in_values=logit[:, tt, :], imm_value=TAKEN)
            link(ins)
            for tt in range(TT):
                nc.vector.tensor_tensor(chosen[:, tt, :], logit_r[:, tt, 0:E], logit[:, tt, 0:E], ALU.is_lt)\
                    .then_inc(s_sel, 1)
            dve.wait_ge(s_sel, TT)
            dve.wait_ge(s_ex, TT)
            link(nc.vector.tensor_tensor(gate_w[:, :, :], gate_w[:, :, :], chosen[:, :, :], ALU.mult))
            link(nc.vector.tensor_reduce(topsum, gate_w[:, :, :], AX_X, ALU.add))
            link(nc.vector.reciprocal(topinv, topsum))
            for tt in range(TT):
                ins = nc.vector.tensor_scalar(gate_w[:, tt, :], gate_w[:, tt, :], topinv[:, tt:tt + 1], None, ALU.mult)
            ins.then_inc(s_w, 1)
            dve.wait_ge(s_w, 1)
            dve.wait_ge(s_pos, 1)
            for tt in range(TT):
                ins = nc.vector.scalar_tensor_tensor(out=place[:, tt, 0:E], in0=bank(7, tt * E, E), scalar=1.0,
                                                     in1=chosen[:, tt, :], op0=ALU.add, op1=ALU.mult)
            link(ins)
            link(nc.vector.tensor_scalar(place[:, :, 0:E], place[:, :, 0:E], -1.0, None, ALU.add))
            link(nc.vector.tensor_reduce(most, bank(7, 2 * E, E), AX_X, ALU.max))
            link(nc.vector.tensor_scalar(rounds_f[:, 0:1], most, float(SLOTS), 1.0, ALU.is_gt, ALU.add))
            for k in range(2):
                link(nc.vector.scalar_tensor_tensor(out=rounds_f[:, k + 1:k + 2], in0=most, scalar=float(SLOTS * (k + 2)),
                                                    in1=rounds_f[:, k:k + 1], op0=ALU.is_gt, op1=ALU.add))
            nc.vector.tensor_copy(rounds_i[:, :], rounds_f[:, 2:3]).then_inc(s_rounds, 1)

            slots1, slots2 = const[:, C_SLOT:C_SLOT + SLOTS], const[:, C_SLOT:C_SLOT + 2 * SLOTS]

            def picks(e):
                for tt in range(TT):
                    nc.vector.tensor_scalar(pick[:, tt, :], slots1, place[:, tt, bass.ds(e, 1)], None, ALU.is_equal)\
                        .then_inc(s_pick, 1)

            def spreads(e):
                for tt in range(TT):
                    nc.vector.tensor_scalar(spread[:, tt, :], slots2, place[:, tt, bass.ds(e, 1)],
                                            gate_w[:, tt, bass.ds(e, 1)], ALU.is_equal, ALU.mult).then_inc(s_spr, 1)

            def take_gathered(gathers):
                dve.wait_ge(s_gat, gathers)
                nc.vector.tensor_tensor(xg[:, :, :], bank(6).rearrange("p (c s) -> p c s", c=DC),
                                        g_moe[:, :].rearrange("p (c o) -> p c o", o=1).to_broadcast([P, DC, SLOTS]),
                                        ALU.mult).then_inc(s_xg, 1)

            def expert_body(e, count, gathers):
                picks(e + 1)
                dve.wait_ge(s_sprt, count)
                spreads(e)
                dve.wait_ge(s_gate, count)
                nc.vector.tensor_scalar(act_g, bank(4), LIMIT, None, ALU.min).then_inc(s_g, 1)
                dve.wait_ge(s_sig, count)
                nc.vector.tensor_tensor(act_s, act_g, act_s, ALU.mult)
                dve.wait_ge(s_up, count)
                ins = nc.vector.tensor_scalar(act_l, bank(5), -LIMIT, LIMIT, ALU.max, ALU.min)
                ins.then_inc(s_lin, 1)
                dve.wait_ge(s_lin, count)
                nc.vector.scalar_tensor_tensor(out=hdn, in0=act_l, scalar=1.0, in1=act_s, op0=ALU.add, op1=ALU.mult)\
                    .then_inc(s_hdn, 1)
                take_gathered(gathers + 1)

            dve.wait_ge(s_rounds, 1)
            picks(0)
            take_gathered(1)
            with dve.Fori(0, E // 2) as i:
                for u in range(2):
                    expert_body(2 * i + u, 2 * i + u + 1, 2 * i + u + 1)
            rounds = dve.value_load(rounds_i[0:1, 0:1], min_val=1, max_val=T // SLOTS)
            with dve.If(rounds > 1):
                with dve.Fori(1, rounds) as r:
                    nc.vector.tensor_scalar(place[:, :, :], place[:, :, :], -float(SLOTS), None, ALU.add)\
                        .then_inc(s_route, 1)
                    dve.wait_ge(s_route, r)
                    picks(0)
                    take_gathered((E + 1) * r + 1)
                    with dve.Fori(0, E // 2) as i:
                        for u in range(2):
                            expert_body(2 * i + u, E * r + 2 * i + u + 1, (E + 1) * r + 2 * i + u + 1)
            dve.wait_ge(s_sq, TT * 5)
            nc.vector.tensor_scalar(var, sumsq, 1.0 / D, EPS, ALU.mult, ALU.add).then_inc(s_var, 1)
            dve.wait_ge(s_std, 5)
            link(nc.vector.reciprocal(rstd, std))
            dve.wait_ge(s_gfin, 16)
            for tt in range(TT):
                nc.vector.scalar_tensor_tensor(out=outp[:, tt, :], in0=bank(2 * tt, 0, D), scalar=rstd[:, tt:tt + 1],
                                               in1=g_fin, op0=ALU.mult, op1=ALU.mult).then_inc(s_out, 1)


_IN = ("x", "mem", "norm_mix", "w_in", "conv_w", "w_branch_attn", "w_branch_conv", "w_gate", "b_gate", "w_out",
       "norm_cross", "norm_mem", "w_cq", "w_ckv", "w_co", "norm_moe", "router_w", "router_b",
       "w_exp_gate", "b_exp_gate", "w_exp_up", "b_exp_up", "w_exp_down", "b_exp_down", "norm_final")


def kernel(**inputs):
    import concourse.bacc as bacc
    from concourse.bass_utils import run_bass_kernel_spmd

    nc = bacc.Bacc("TRN2", target_bir_lowering=False, num_devices=1)
    arrays, io = {}, {}
    for name in _IN:
        a = np.ascontiguousarray(inputs[name])
        if name != "norm_final":
            a = a.reshape(a.shape[1:])
        if name == "conv_w":
            a = a.reshape(-1)
        arrays[f"in_{name}"] = a
    arrays["in_const"] = constants()
    for key, a in arrays.items():
        io[key[3:]] = nc.dram_tensor(key, a.shape, F32, kind="ExternalInput").ap()
    io["out"] = nc.dram_tensor("out_h", (T, D), F32, kind="ExternalOutput").ap()
    build(nc, io)
    r = run_bass_kernel_spmd(nc, [arrays], core_ids=[0])
    return r.results[0]["out_h"].reshape(inputs["x"].shape)
```

```python
from contextlib import ExitStack

import numpy as np

import concourse.bass as bass
from concourse import mybir

F32 = mybir.dt.float32
F32R = mybir.dt.float32r
I32 = mybir.dt.int32
ALU = mybir.AluOpType
ACT = mybir.ActivationFunctionType
AX_X = mybir.AxisListType.X

P = 128
T, D = 256, 1024
TT = T // P
DC = D // P
GROUPS, HEADS, HD = 3, 8, 64
AW = HEADS * HD
DILATION = (1, 4, 16)
WINDOW_STEPS = 128
PAIRS = HEADS // 2
CONV_K = 3
MH, MHD = 4, 128
E, TOPK, FF = 32, 4, 1024
SLOTS = 64
LIMIT, ALPHA, EPS = 7.0, 1.702, 1e-6
SENTINEL, TAKEN = -3.0e38, -3.3e38
MASKED = 1e30

KEYS1, KEYS0 = GROUPS * T, GROUPS * P
SCORES = KEYS1 + KEYS0
BLOCKS = SCORES // P

C_IDENT = 0
C_DIST = C_IDENT + P
C_BEFORE = C_DIST + SCORES
C_ONES = C_BEFORE + P
C_SLOT = C_ONES + P
C_PICK = C_SLOT + 2 * SLOTS
C_SLOPE = C_PICK + 3 * SLOTS
C_ALL = C_SLOPE + HEADS

V_MEM, V_MIX, V_CROSS = 0, DC, 2 * DC
V_BGATE = 3 * DC
V_CONV = V_BGATE + 2 * DC
V_ALL = V_CONV + CONV_K * DC


def constants():
    c = np.zeros((P, C_ALL), np.float32)
    c[:, C_IDENT:C_IDENT + P] = np.eye(P)
    q, k = np.arange(T)[:, None], np.arange(T)[None, :]
    for g, dil in enumerate(DILATION):
        d = q - k
        ok = (d >= 0) & (d % dil == 0) & (d <= WINDOW_STEPS * dil)
        dist = np.where(ok, d, MASKED).astype(np.float32)
        c[:, C_DIST + g * T:C_DIST + (g + 1) * T] = dist[P:, :]
        c[:, C_DIST + KEYS1 + g * P:C_DIST + KEYS1 + (g + 1) * P] = dist[:P, :P]
    c[:, C_BEFORE:C_BEFORE + P] = np.arange(P)[:, None] < np.arange(P)[None, :]
    c[:, C_ONES:C_ONES + P] = 1.0
    c[:, C_SLOT:C_SLOT + 2 * SLOTS] = np.tile(np.arange(SLOTS), 2)[None, :]
    for r in range(3):
        c[r, C_PICK + r * SLOTS:C_PICK + (r + 1) * SLOTS] = 1.0
    c[:, C_SLOPE:C_SLOPE + HEADS] = -(2.0 ** -np.arange(1.0, HEADS + 1)) * HD ** 0.5
    return c


def build(nc, io):
    ctx = ExitStack()
    with ctx:
        def sb(name, shape, dt=F32):
            return ctx.enter_context(nc.sbuf_tensor(name, shape, dt))

        def sem(name):
            return ctx.enter_context(nc.semaphore(name))

        SLOT_N = DC * 512
        ring = sb("ring", [P, 6 * SLOT_N])
        ring_at = nc.sbuf_base - 6 * SLOT_N * 4

        def slot(s):
            return ring[:, s * SLOT_N:(s + 1) * SLOT_N]

        const = sb("const", [P, C_ALL])
        ident = const[:, C_IDENT:C_IDENT + P]
        h = sb("h", [P, TT, D])
        xT = sb("xT", [P, DC, T])
        xT_at = nc.sbuf_base - DC * T * 4
        ycT = sb("ycT", [P, DC, T])
        memT = ycT
        qk = sb("qk", [P, 2, GROUPS, PAIRS, T])
        v = sb("v", [P, GROUPS, TT, AW])
        gates = sb("gates", [P, 2, DC, T])
        kmT = sb("kmT", [P, MH, T])
        vm = sb("vm", [P, TT, MH * MHD])
        prob = sb("prob", [P, SCORES])
        probT = sb("probT", [P, BLOCKS, P])
        ya = sb("ya", [P, TT, AW])
        vecs = sb("vecs", [P, V_ALL])
        small = sb("small", [P, 64])
        wr = sb("wr", [P, DC, E])
        rb = sb("rb", [P, E])
        g_moe = sb("g_moe", [P, DC])
        rounds_i = sb("rounds_i", [P, 1], I32)

        mem_in = v[:, :, :, :].rearrange("p g a n -> p (g a n)")[:, 0:TT * D].rearrange("p (a d) -> p a d", a=TT)
        flat_qk = qk[:, :, :, :, :].rearrange("p u g a t -> p (u g a t)")
        normed = flat_qk[:, 0:TT * D].rearrange("p (a d) -> p a d", a=TT)
        vec_rows = prob[0:V_ALL, 0:P]
        PIECE_N = DC * 256
        land = [ring[:, n * PIECE_N:(n + 1) * PIECE_N].rearrange("p (c n) -> p c n", c=DC) for n in range(6)]
        cut = nc.alloc_sbuf_tensor_at("cut", [P, 2, 2, DC, 256], F32R, offset=ring_at + 3 * SLOT_N * 4)
        xT_hi = nc.alloc_sbuf_tensor_at("xT_hi", [P, DC, T], F32R, offset=xT_at)
        xT_lo = nc.alloc_sbuf_tensor_at("xT_lo", [P, DC, T], F32R, offset=ring_at + 5 * SLOT_N * 4 + 2048 * 4)
        x_part = (xT_hi, xT_lo)
        spare = ring[:, 5 * SLOT_N:5 * SLOT_N + 2048]
        x_whole = gates[:, :, :, :].rearrange("p a c t -> p (a c t)")[:, 0:DC * T].rearrange("p (c t) -> p c t", c=DC)
        stage_q = spare[:, 0:2 * GROUPS * T].rearrange("p (u g t) -> p u g t", u=2, g=GROUPS)
        gb_sb = spare[:, 2 * GROUPS * T:2 * GROUPS * T + 2 * T].rearrange("p (a t) -> p a t", a=2)
        gc_sb = sb("gc_sb", [P, 2, T])
        conv_z = sb("conv_z", [P, 2, T + CONV_K - 1])
        mixT = flat_qk[:, TT * D:TT * D + DC * T].rearrange("p (c t) -> p c t", c=DC)
        yaT = flat_qk[:, TT * D + DC * T:TT * D + (DC + 4) * T].rearrange("p (j t) -> p j t", j=4)
        mix_a = gc_sb[:, :, :]
        mix_b = conv_z[:, :, 0:T]
        flat_v = v[:, :, :, :].rearrange("p g a n -> p (g a n)")
        qcT = flat_v[:, 0:MH * T].rearrange("p (m t) -> p m t", m=MH)
        ocT = flat_v[:, MH * T:2 * MH * T].rearrange("p (a m t) -> p a m t", a=TT, m=MH)
        flat_g = gates[:, :, :, :].rearrange("p a c t -> p (a c t)")
        pc = flat_g[:, 0:TT * MH * T].rearrange("p (a m k) -> p a m k", a=TT, m=MH)
        pcT = flat_g[:, TT * MH * T:2 * TT * MH * T].rearrange("p (a m b t) -> p a m b t", a=TT, m=MH, b=TT)

        logit = sb("logit", [P, TT, E + 4])
        top8 = sb("top8", [P, TT, 8])
        wanted = sb("wanted", [P, TT, 8])
        flat_pt = probT[:, :, :].rearrange("p b q -> p (b q)")
        logit_r = flat_pt[:, 0:TT * (E + 4)].rearrange("p (a e) -> p a e", a=TT)
        chosen = flat_pt[:, 128:128 + TT * E].rearrange("p (a e) -> p a e", a=TT)
        gate_w = flat_pt[:, 256:256 + TT * E].rearrange("p (a e) -> p a e", a=TT)
        place = sb("place", [P, TT, E + 2])
        f = 0

        def region(n):
            nonlocal f
            f += n
            assert f <= 2 * DC * T
            return flat_g[:, f - n:f]

        act_g = region(512)
        act_s = region(512)
        act_l = region(512)
        hdn = region(512)
        hdnT = region(512).rearrange("p (j s) -> p j s", j=4)
        y_sb = region(512)
        spread = region(2 * P).rearrange("p (a s) -> p a s", a=TT)
        spreadT = region(2 * P).rearrange("p (a t) -> p a t", a=TT)
        xg = prob[:, 0:DC * SLOTS].rearrange("p (c s) -> p c s", c=DC)
        pick = prob[:, DC * SLOTS:DC * SLOTS + TT * SLOTS].rearrange("p (a s) -> p a s", a=TT)
        bias = [flat_v[:, u * D:(u + 1) * D] for u in range(2)]
        more_slots = (flat_qk[:, TT * D:TT * D + SLOT_N],
                      nc.alloc_sbuf_tensor_at("slot7", [P, SLOT_N], F32, offset=xT_at)[:, :])
        outp = normed
        g_fin = flat_v[:, 2 * MH * T:2 * MH * T + D]

        ps = ctx.enter_context(nc.psum_tensor("ps", [P, 8 * 512], F32))

        def bank(b, lo=0, n=512):
            return ps[:, b * 512 + lo:b * 512 + lo + n]

        sumsq, var, std, rstd = (small[:, 2 * k:2 * k + 2] for k in range(4))
        nmax = small[:, 8:12].rearrange("p (u a) -> p u a", u=2)
        psum_ = small[:, 12:16].rearrange("p (u a) -> p u a", u=2)
        rinv = small[:, 16:20].rearrange("p (u a) -> p u a", u=2)
        rowmax = small[:, 20:22]
        cmax, cneg, csum, cinv = (small[:, 22 + 8 * k:30 + 8 * k].rearrange("p (a m) -> p a m", a=TT)
                                  for k in range(4))
        topneg, topsum, topinv = (small[:, 54 + 2 * k:56 + 2 * k] for k in range(3))
        most = small[:, 60:61]
        rounds_f = small[:, 61:64]

        s_ident, s_const, s_vec, s_x, s_mem, s_wr, s_bd, s_gfin = (sem(n) for n in (
            "ident_loaded", "const_loaded", "vec_loaded", "x_loaded", "mem_loaded", "router_loaded", "down_bias_loaded", "final_gain_loaded"))
        s_ckv = [sem(f"ckv_loaded{n}") for n in range(2)]
        s_land = [sem(f"piece_loaded{n}") for n in range(6)]
        s_hi, s_lo = sem("hi_parts_ready"), sem("lo_parts_ready")
        s_xhi, s_xlo = sem("x_hi_ready"), sem("x_lo_ready")
        s_branch = sem("w_branch_loaded")
        s_wout = [sem(f"w_out_loaded{n}") for n in range(2)]
        s_cq, s_co = sem("w_cq_loaded"), sem("w_co_loaded")
        s_slot = [sem(f"expert_part_loaded{n}") for n in range(8)]
        s_bias = [sem(f"bias_loaded{n}") for n in range(2)]
        s_half = sem("first_half_used")
        s_zero = sem("zeros_written")
        s_dve = sem("vector_step")
        s_act = sem("scalar_step")
        s_vecT, s_vecs = sem("vec_turned"), sem("vec_ready")
        s_sq, s_var, s_std, s_nrm, s_trn, s_xT = (sem(n) for n in (
            "sumsq_ready", "var_ready", "std_ready", "normed_ready", "normed_turned", "xT_ready"))
        s_unit, s_evac = sem("projection_ready"), sem("projection_copied")
        s_stage, s_score, s_scread = sem("q_staged"), sem("scores_ready"), sem("scores_read")
        s_nmax, s_prob, s_ptp, s_pt = (sem(n) for n in (
            "max_ready", "prob_ready", "prob_turned", "probT_ready"))
        s_pv, s_ya = sem("attn_out_ready"), sem("ya_ready")
        s_xc, s_conv = sem("xc_used"), sem("conv_done")
        s_yat, s_yaT = sem("ya_turned"), sem("yaT_ready")
        s_mixp, s_mixread, s_mix = sem("branch_ready"), sem("branch_read"), sem("mix_ready")
        s_hp, s_h = sem("h_addend_ready"), sem("h_ready")
        s_cs, s_cm, s_ce, s_cn, s_ct, s_cpt, s_cv, s_co_t = (sem(n) for n in (
            "cross_scores", "cross_max", "cross_exp", "cross_prob", "cross_turned", "cross_probT",
            "cross_out", "cross_outT"))
        s_w = sem("token_weights_ready")
        s_lg, s_top, s_ex, s_sel, s_pos, s_route = (sem(n) for n in (
            "logits_ready", "top_ready", "top_exp_ready", "chosen_ready", "positions_ready", "routes_ready"))
        s_rounds = sem("rounds_ready")
        s_pick, s_gat, s_xg = sem("pick_ready"), sem("gathered"), sem("xg_ready")
        s_gate, s_g, s_sig, s_up, s_lin, s_hdn = (sem(n) for n in (
            "gate_ready", "gate_clamped", "sigmoid_ready", "up_ready", "up_clamped", "hdn_ready"))
        s_spr, s_sprt, s_sprT = sem("spread_ready"), sem("spread_turned"), sem("spreadT_ready")
        s_ht, s_hT, s_y, s_ysb, s_sum = (sem(n) for n in (
            "hdn_turned", "hdnT_ready", "y_ready", "y_copied", "sum_updated"))
        s_out = sem("out_ready")
        s_store = sem("out_stored")

        FREE = 1
        UNITS_A = 6 * GROUPS
        UNITS_B = UNITS_A + 5 * PAIRS
        UNITS_M = UNITS_B + 4
        COPIED_B = 2 + UNITS_A + 4 * PAIRS
        RING = (3, 4, 6, 1, 2, 5, 0, 7)

        def part_place(w, k, fours=0):
            n = 6 * w + k
            return RING[n % len(RING)], 3 * fours + n // len(RING) + 1


        w_in = io["w_in"].rearrange("(c p) n -> p c n", p=P)
        w_gate = io["w_gate"].rearrange("(c p) n -> p c n", p=P)
        w_in_q = io["w_in"].rearrange("(c p) (q n) -> q p c n", p=P, n=256)
        w_gate_q = io["w_gate"].rearrange("(c p) (q n) -> q p c n", p=P, n=256)
        CONV0 = GROUPS * 3 * AW

        def cols(s, n=512):
            return slot(s)[:, 0:DC * n].rearrange("p (c n) -> p c n", c=DC)

        def rows(s):
            return (slot(s) if s < 6 else more_slots[s - 6]).rearrange("p (c n) -> p c n", c=4)

        block = ctx.enter_context(nc.Block())

        def load_expert(sp, w, e, free):
            wg = io["w_exp_gate"][bass.ds(e, 1)].rearrange("e (p c) n -> p (e c) n", c=DC)
            wu = io["w_exp_up"][bass.ds(e, 1)].rearrange("e (p c) n -> p (e c) n", c=DC)
            wd = io["w_exp_down"][bass.ds(e, 1)].rearrange("e (b p j) n -> p b (e j) n", b=2, j=4)
            parts = [wg[:, 0:4, :], wg[:, 4:8, :], wu[:, 0:4, :], wu[:, 4:8, :], wd[:, 0, :, :], wd[:, 1, :, :]]
            for k in range(6):
                place_, _ = part_place(w, k)
                sp.wait_ge(*free[k])
                sp.dma_start(rows(place_), parts[k]).then_inc(s_slot[place_], 16)

        def eight_before(e):
            return ((s_half, 3 * e - 3), (s_y, e - 1), (s_half, 3 * e - 2), (s_gate, e),
                    (s_half, 3 * e - 1), (s_up, e))

        @block.sync
        def _(sp):
            sp.dma_start(h[:, :, :], io["x"].rearrange("(a p) d -> p a d", p=P)).then_inc(s_x, 16)
            sp.dma_start(ident, io["const"][:, 0:P]).then_inc(s_ident, 16)
            for row, name, n in ((V_MEM, "norm_mem", DC), (V_MIX, "norm_mix", DC), (V_CROSS, "norm_cross", DC),
                                 (V_BGATE, "b_gate", 2 * DC), (V_CONV, "conv_w", CONV_K * DC)):
                sp.dma_start(vec_rows[row:row + n, :], io[name].rearrange("(a n) -> a n", n=P)).then_inc(s_vec, 16)
            for n in range(6):
                sp.dma_start(land[n], w_in_q[n]).then_inc(s_land[n], 16)
            sp.dma_start(const[:, P:], io["const"][:, P:]).then_inc(s_const, 16)
            sp.dma_start(wr[:, :, :], io["router_w"].rearrange("(p c) e -> p c e", c=DC)).then_inc(s_wr, 16)
            sp.dma_start(rb[:, :], io["router_b"].rearrange("(a e) -> a e", a=1).to_broadcast([P, E])).then_inc(s_wr, 16)
            sp.dma_start(g_moe[:, :], io["norm_moe"].rearrange("(p c) -> p c", c=DC)).then_inc(s_wr, 16)
            with sp.Fori(0, GROUPS - 1) as g:
                for n in range(6):
                    sp.wait_ge(s_lo, 2 * (6 * g + n) + 2)
                    sp.dma_start(land[n], w_in_q[bass.ds(6 * g + 6 + n, 1)].rearrange("q p c n -> p (q c) n"))\
                        .then_inc(s_land[n], 16)

            def load_pieces(i, cut_before):
                for n in range(5):
                    src = w_in_q[bass.ds(CONV0 // 256 + 4 * n + i, 1)] if n < 3 else \
                        w_gate_q[bass.ds(4 * (n - 3) + i, 1)]
                    sp.wait_ge(s_lo, cut_before(n))
                    sp.dma_start(land[n], src.rearrange("q p c n -> p (q c) n")).then_inc(s_land[n], 16)

            load_pieces(0, lambda n: 2 * (6 * GROUPS - 6 + n) + 2)
            with sp.Fori(0, PAIRS - 1) as i:
                load_pieces(i + 1, lambda n: 2 * (6 * GROUPS + 5 * i + n) + 2)
            sp.wait_ge(s_lo, 2 * UNITS_B - 6)
            sp.dma_start(rows(0), io["w_branch_attn"].rearrange("(c p) n -> p c n", p=P)).then_inc(s_branch, 16)
            for n in range(2):
                sp.wait_ge(s_lo, 2 * UNITS_B - 2 + 2 * n)
                sp.dma_start(rows(1 + n), io["w_branch_conv"].rearrange("(b c p) n -> b p c n", b=2, p=P)[n])\
                    .then_inc(s_branch, 16)
            sp.wait_ge(s_unit, 2 + UNITS_B)
            sp.dma_start(mem_in, io["mem"].rearrange("(a p) d -> p a d", p=P)).then_inc(s_mem, 16)
            for n in range(2):
                sp.dma_start(cols(3 + n), io["w_out"].rearrange("(c p) n -> p c n", p=P)[:, :, n * 512:(n + 1) * 512])\
                    .then_inc(s_wout[n], 16)
            sp.wait_ge(s_conv, FREE + PAIRS)
            sp.dma_start(cols(5), io["w_cq"].rearrange("(c p) n -> p c n", p=P)).then_inc(s_cq, 16)
            sp.wait_ge(s_mixp, DC)
            for n in range(2):
                sp.dma_start(cols(1 + n), io["w_ckv"].rearrange("(c p) n -> p c n", p=P)[:, :, n * 512:(n + 1) * 512])\
                    .then_inc(s_ckv[n], 16)
            sp.dma_start(rows(0), io["w_co"].rearrange("(c p) n -> p c n", p=P)).then_inc(s_co, 16)
            first = ((s_hp, 2), (s_hp, 4), (s_hp, 4), (s_unit, 2 + UNITS_B + 2), (s_unit, 2 + UNITS_M),
                     (s_unit, 2 + UNITS_M + 2), (s_hp, 4 + 2 * TT), (s_lg, 1))
            load_expert(sp, 0, 0, first[0:6])
            load_expert(sp, 1, 1, first[6:8] + eight_before(1)[2:])
            for w in range(2, 4):
                load_expert(sp, w, w, eight_before(w))
            with sp.Fori(1, E // 4) as i:
                for w in range(4):
                    load_expert(sp, w, 4 * i + w, eight_before(4 * i + w))
            sp.wait_ge(s_rounds, 1)
            rounds = sp.value_load(rounds_i[0:1, 0:1], min_val=1, max_val=T // SLOTS)
            with sp.If(rounds > 1):
                with sp.Fori(1, rounds) as r:
                    with sp.Fori(0, E // 4) as i:
                        for w in range(4):
                            load_expert(sp, w, 4 * i + w, eight_before(E * r + 4 * i + w))
            for tt in range(TT):
                sp.wait_ge(s_out, tt + 1)
                sp.dma_start(io["out"][tt * P:(tt + 1) * P, :], outp[:, tt, :]).then_inc(s_store, 16)
            sp.wait_ge(s_store, 16 * TT)

        @block.gpsimd
        def _(pool):
            nc.gpsimd.memset(stage_q, 0.0).then_inc(s_zero, 1)
            nc.gpsimd.memset(conv_z[:, :, 0:CONV_K - 1], 0.0).then_inc(s_zero, 1)
            nc.gpsimd.memset(logit[:, :, E:E + 4], SENTINEL).then_inc(s_zero, 1)
            nc.gpsimd.memset(wanted[:, :, 4:8], SENTINEL).then_inc(s_zero, 1)
            nc.gpsimd.memset(place[:, :, E:E + 2], -1.0).then_inc(s_zero, 1)
            pool.wait_ge(s_zero, 5)
            pool.wait_ge(s_evac, 2 + UNITS_A)
            with pool.Fori(0, PAIRS) as i:
                for u in range(2):
                    rs = slice(u * HD, (u + 1) * HD)
                    pool.wait_ge(s_score, 2 * i + u + 1)
                    nc.gpsimd.tensor_copy(stage_q[rs, u, :, :], qk[rs, 0, :, bass.ds(i, 1), :]).then_inc(s_stage, 1)
                    pool.wait_ge(s_stage, 2 * i + u + 1)
            pool.wait_ge(s_hp, 4 + 2 * TT)
            for u in range(2):
                nc.gpsimd.memset(bias[u], 0.0).then_inc(s_zero, 1)
            nc.gpsimd.memset(y_sb, 0.0).then_inc(s_zero, 1)
            nc.gpsimd.memset(spread[:, :, :], 0.0).then_inc(s_zero, 1)
            pool.wait_ge(s_zero, 9)
            for half in range(2):
                pool.dma_start(y_sb[half * SLOTS:half * SLOTS + E, :],
                               io["b_exp_down"][:, half * 512:(half + 1) * 512]).then_inc(s_bd, 16)

            def load_bias(u, e):
                for k, name in enumerate(("b_exp_gate", "b_exp_up")):
                    pool.dma_start(bias[u][k:k + 1, :], io[name][bass.ds(e, 1), :]).then_inc(s_bias[u], 16)

            for u in range(2):
                load_bias(u, u)
            with pool.Fori(1, E // 2) as i:
                for u in range(2):
                    pool.wait_ge(s_up, 2 * i + u - 1)
                    load_bias(u, 2 * i + u)
            pool.wait_ge(s_rounds, 1)
            rounds = pool.value_load(rounds_i[0:1, 0:1], min_val=1, max_val=T // SLOTS)
            with pool.If(rounds > 1):
                with pool.Fori(1, rounds) as r:
                    with pool.Fori(0, E // 2) as i:
                        for u in range(2):
                            pool.wait_ge(s_up, E * r + 2 * i + u - 1)
                            load_bias(u, 2 * i + u)

        @block.tensor
        def _(pe):
            def turn_vectors():
                pe.wait_ge(s_ident, 16)
                pe.wait_ge(s_vec, 16 * 5)
                nc.tensor.transpose(bank(2, 0, V_ALL), vec_rows, ident[0:V_ALL, 0:V_ALL]).then_inc(s_vecT, 1)

            def turn_normed(k):
                for tt in range(TT):
                    pe.wait_ge(s_nrm, TT * k + tt + 1)
                    for c in range(DC):
                        last = nc.tensor.transpose(bank(4 + 2 * tt, c * P, P), normed[:, tt, c * P:(c + 1) * P], ident)
                    last.then_inc(s_trn, 1)

            def project_T(b, w, c0, src):
                for j in range(2):
                    for c in range(DC):
                        last = nc.tensor.matmul(bank(b, j * T, T), w[:, c, c0 + j * P:c0 + (j + 1) * P], src[:, c, :],
                                                start=(c == 0), stop=(c == DC - 1))
                return last

            def project(b, w, tt, src):
                for c in range(DC):
                    last = nc.tensor.matmul(bank(b), src[:, c, tt * P:(tt + 1) * P], w[:, c, :],
                                            start=(c == 0), stop=(c == DC - 1))
                return last

            pe.nop().then_inc(s_score, 2)
            pe.nop().then_inc(s_unit, 2)
            turn_vectors()
            turn_normed(0)
            PARTS = ((0, 0), (0, 1), (1, 0))

            def project_cut(b, k, transposed, cut_before):
                for j in range(2):
                    for half in range(2):
                        if j == 0:
                            pe.wait_ge(s_lo, cut_before + half + 1)
                        for c in range(4 * half, 4 * half + 4):
                            for wp, xp in PARTS:
                                w, x = cut[:, k, wp, c, :], x_part[xp][:, c, :]
                                s_, m_ = (w[:, j * P:(j + 1) * P], x) if transposed else (x[:, j * P:(j + 1) * P], w)
                                last = nc.tensor.matmul(bank(b, j * T, T), s_, m_, start=(c == 0 and wp + xp == 0),
                                                        stop=(c == DC - 1 and wp == 1))
                return last

            pe.wait_ge(s_xhi, TT)
            pe.wait_ge(s_xlo, TT)
            with pe.Fori(0, GROUPS) as g:
                for n in range(6):
                    pe.wait_ge(s_evac, 6 * g + n + 1)
                    project_cut(n % 2, n % 2, n < 4, 12 * g + 2 * n).then_inc(s_unit, 1)

            def scores(i, u):
                pe.wait_ge(s_stage, 2 * i + u + 1)
                pe.wait_ge(s_scread, FREE + 2 * i + u)
                for g in range(GROUPS):
                    nc.tensor.matmul(ps[:, 2 * 512 + g * T:2 * 512 + (g + 1) * T], stage_q[:, u, g, P:T],
                                     qk[:, 1, g, bass.ds(i, 1), :], start=True, stop=True)
                for g in range(GROUPS):
                    last = nc.tensor.matmul(bank(4, g * P, P), stage_q[:, u, g, 0:P],
                                            qk[:, 1, g, bass.ds(i, 1), 0:P], start=True, stop=True)
                last.then_inc(s_score, 1)

            def turn_probs(i, u):
                pe.wait_ge(s_prob, 2 * (2 * i + u) + 2)
                pe.wait_ge(s_ya, FREE + 2 * i + u)
                for b in range(BLOCKS):
                    last = nc.tensor.transpose(bank(5, b * P, P), prob[:, b * P:(b + 1) * P], ident)
                last.then_inc(s_ptp, 1)

            def attend(i, u):
                pe.wait_ge(s_pt, 2 * i + u + 1)
                for tt, (b0, kts) in enumerate(((2 * GROUPS, 1), (0, 2))):
                    for g in range(GROUPS):
                        for kt in range(kts):
                            last = nc.tensor.matmul(
                                bank(7, 256 + tt * HD, HD), probT[:, b0 + g * kts + kt, :],
                                v[:, g, kt, bass.ds(2 * HD * i + u * HD, HD)],
                                start=(g == 0 and kt == 0), stop=(g == GROUPS - 1 and kt == kts - 1))
                last.then_inc(s_pv, 1)

            def unit(i, n, k):
                if n == 4:
                    pe.wait_ge(s_xc, i + 1)
                elif n == 3:
                    pe.wait_ge(s_evac, 2 + UNITS_A + 4 * i + 2)
                else:
                    pe.wait_ge(s_evac, 2 + UNITS_A + 4 * i - 1 + n)
                project_cut(k, k, True, 2 * (UNITS_A + 5 * i + n)).then_inc(s_unit, 1)

            with pe.Fori(0, PAIRS // 2) as ii:
                for q in range(2):
                    i = 2 * ii + q
                    scores(i, 0)
                    unit(i, 0, q)
                    turn_probs(i, 0)
                    scores(i, 1)
                    unit(i, 1, 1 - q)
                    attend(i, 0)
                    unit(i, 2, q)
                    turn_probs(i, 1)
                    unit(i, 3, 1 - q)
                    attend(i, 1)
                    unit(i, 4, q)

            pe.wait_ge(s_ya, FREE + HEADS)
            for j in range(4):
                for tt in range(TT):
                    last = nc.tensor.transpose(bank(2, j * T + tt * P, P), ya[:, tt, j * P:(j + 1) * P], ident)
            last.then_inc(s_yat, 1)
            pe.wait_ge(s_branch, 16 * 3)
            pe.wait_ge(s_yaT, 1)
            pe.wait_ge(s_conv, FREE + PAIRS)
            pe.wait_ge(s_evac, COPIED_B)
            for m in range(DC):
                if m >= 2:
                    pe.wait_ge(s_mixread, m - 1)
                for c in range(4):
                    nc.tensor.matmul(bank(m % 2, 0, T), rows(0)[:, c, m * P:(m + 1) * P], yaT[:, c, :],
                                     start=(c == 0), stop=(c == 3))
                for c in range(DC):
                    last = nc.tensor.matmul(bank(m % 2, T, T), rows(1 + c // 4)[:, c % 4, m * P:(m + 1) * P],
                                            ycT[:, c, :], start=(c == 0), stop=(c == DC - 1))
                last.then_inc(s_mixp, 1)
            turn_normed(1)
            pe.wait_ge(s_mix, DC)
            for half in range(2):
                pe.wait_ge(s_wout[half], 16)
                if half:
                    pe.wait_ge(s_xT, 2 * TT)
                for tt in range(TT):
                    project(2 + 2 * half + tt, cols(3 + half), tt, mixT).then_inc(s_hp, 1)
            pe.wait_ge(s_ckv[0], 16)
            pe.wait_ge(s_xT, 2 * TT)
            pe.wait_ge(s_mixread, DC)
            for j in range(2):
                project_T(j, cols(1), j * 256, memT).then_inc(s_unit, 1)
            pe.wait_ge(s_ckv[1], 16)
            for tt in range(TT):
                pe.wait_ge(s_evac, COPIED_B + tt + 1)
                project(tt, cols(2), tt, memT).then_inc(s_unit, 1)

            turn_normed(2)
            pe.wait_ge(s_cq, 16)
            pe.wait_ge(s_xT, 3 * TT)
            for j in range(2):
                pe.wait_ge(s_evac, COPIED_B + 3 + j)
                project_T(j, cols(5), j * 256, xT).then_inc(s_unit, 1)
            pe.wait_ge(s_evac, COPIED_B + 6)
            for tt in range(TT):
                for m in range(MH):
                    last = nc.tensor.matmul(bank(2 + 2 * tt, m * T, T), qcT[:, m, tt * P:(tt + 1) * P], kmT[:, m, :],
                                            start=True, stop=True)
                last.then_inc(s_cs, 1)
            for tt in range(TT):
                pe.wait_ge(s_cn, tt + 1)
                for m in range(MH):
                    for b in range(TT):
                        last = nc.tensor.transpose(bank((6, 2)[tt], (m * TT + b) * P, P),
                                                   pc[:, tt, m, b * P:(b + 1) * P], ident)
                last.then_inc(s_ct, 1)
                pe.wait_ge(s_cpt, tt + 1)
                for m in range(MH):
                    for b in range(TT):
                        last = nc.tensor.matmul(bank(tt, m * P, P), vm[:, b, m * MHD:(m + 1) * MHD],
                                                pcT[:, tt, m, b, :], start=(b == 0), stop=(b == TT - 1))
                last.then_inc(s_cv, 1)
            pe.wait_ge(s_co, 16)
            for tt in range(TT):
                pe.wait_ge(s_co_t, tt + 1)
                for half in range(2):
                    for m in range(MH):
                        last = nc.tensor.matmul(bank(4 + 2 * tt + half), ocT[:, tt, m, :],
                                                rows(0)[:, m, half * 512:(half + 1) * 512],
                                                start=(m == 0), stop=(m == MH - 1))
                    last.then_inc(s_hp, 1)

            pe.wait_ge(s_h, 2 * 2 * TT)
            for tt in range(TT):
                for half in range(2):
                    last = nc.tensor.matmul(bank(2 * tt + half), ident, h[:, tt, half * 512:(half + 1) * 512],
                                            start=True, stop=False, skip_group_check=True)
            turn_normed(3)
            pe.wait_ge(s_xT, 4 * TT)
            pe.wait_ge(s_wr, 48)
            for tt in range(TT):
                for c in range(DC):
                    last = nc.tensor.matmul(bank(6, tt * E, E), xT[:, c, tt * P:(tt + 1) * P], wr[:, c, :],
                                            start=(c == 0), stop=(c == DC - 1))
            last.then_inc(s_lg, 1)
            pe.wait_ge(s_sel, TT)
            before, ones = const[:, C_BEFORE:C_BEFORE + P], const[:, C_ONES:C_ONES + P]
            nc.tensor.matmul(bank(7, 0, E), before, chosen[:, 0, :], start=True, stop=True)
            nc.tensor.matmul(bank(7, E, E), ones, chosen[:, 0, :], start=True, stop=False)
            nc.tensor.matmul(bank(7, E, E), before, chosen[:, 1, :], start=False, stop=True)
            nc.tensor.matmul(bank(7, 2 * E, E), ones, chosen[:, 0, :], start=True, stop=False)
            nc.tensor.matmul(bank(7, 2 * E, E), ones, chosen[:, 1, :], start=False, stop=True).then_inc(s_pos, 1)

            pe.wait_ge(s_w, 1)
            for tt in range(TT):
                last = nc.tensor.transpose(bank(4, tt * P, P), spread[:, tt, :], ident)
            last.then_inc(s_sprt, 1)

            def gather(count):
                pe.wait_ge(s_pick, 2 * count)
                for c in range(DC):
                    for tt in range(TT):
                        last = nc.tensor.matmul(bank(6, c * SLOTS, SLOTS), normed[:, tt, c * P:(c + 1) * P],
                                                pick[:, tt, :], start=(tt == 0), stop=(tt == TT - 1))
                last.then_inc(s_gat, 1)

            def wide(b, k0, w, fours, w0, row):
                for half in range(2 if row is not None else 0):
                    nc.tensor.matmul(bank(b)[half * SLOTS:(half + 1) * SLOTS, :],
                                     const[:, C_PICK + row * SLOTS:C_PICK + (row + 1) * SLOTS],
                                     bias[w % 2][:, half * 512:(half + 1) * 512], start=True, stop=False)
                for part in range(2):
                    s, landed = part_place(w, k0 + part, fours)
                    pe.wait_ge(s_slot[s], 16 * landed)
                    for j in range(4):
                        for half in range(2):
                            last = nc.tensor.matmul(bank(b)[half * SLOTS:(half + 1) * SLOTS, :],
                                                    w0(part, j), rows(s)[:, j, half * 512:(half + 1) * 512],
                                                    start=(row is None and part == 0 and j == 0),
                                                    stop=(part == 1 and j == 3))
                    if part == 0:
                        last.then_inc(s_half, 1)
                return last

            def add_rows():
                for tt in range(TT):
                    for half in range(2):
                        rs = slice(half * SLOTS, (half + 1) * SLOTS)
                        last = nc.tensor.matmul(bank(2 * tt + half), spreadT[rs, tt, :], y_sb[rs, :],
                                                start=False, stop=False, skip_group_check=True)
                return last

            def expert_body(w, fours, count, gathers):
                pe.wait_ge(s_xg, gathers)
                pe.wait_ge(s_bias[w % 2], 64 * fours + 32 * (w // 2 + 1))
                pe.wait_ge(s_sprT, count)
                wide(4, 0, w, fours, lambda part, j: xg[:, 4 * part + j, :], 0).then_inc(s_gate, 1)
                gather(gathers + 1)
                wide(5, 2, w, fours, lambda part, j: xg[:, 4 * part + j, :], 1).then_inc(s_up, 1)
                pe.wait_ge(s_ysb, count)
                add_rows()
                pe.wait_ge(s_hdn, count)
                pe.wait_ge(s_xg, gathers + 1)
                for j in range(4):
                    last = nc.tensor.transpose(bank(6, j * P, P),
                                               hdn.rearrange("p (n j) -> p j n", j=4)[:, j, :], ident)
                last.then_inc(s_ht, 1)
                pe.wait_ge(s_spr, 2 * count)
                pe.wait_ge(s_g, count)
                for tt in range(TT):
                    last = nc.tensor.transpose(bank(4, tt * P, P), spread[:, tt, :], ident)
                last.then_inc(s_sprt, 1)
                pe.wait_ge(s_hT, count)
                wide(7, 4, w, fours, lambda part, j: hdnT[:, j, part * SLOTS:(part + 1) * SLOTS], None).then_inc(s_y, 1)

            def last_rows(count):
                pe.wait_ge(s_sprT, FREE + count)
                pe.wait_ge(s_ysb, FREE + count)

            gather(1)
            pe.wait_ge(s_bd, 32)
            with pe.Fori(0, E // 4) as i:
                for w in range(4):
                    expert_body(w, i, 4 * i + w + 1, 4 * i + w + 1)
            last_rows(E)
            pe.wait_ge(s_rounds, 1)
            rounds = pe.value_load(rounds_i[0:1, 0:1], min_val=1, max_val=T // SLOTS)
            with pe.If(rounds > 1):
                with pe.Fori(1, rounds) as r:
                    gather((E + 1) * r + 1)
                    with pe.Fori(0, E // 4) as i:
                        for w in range(4):
                            expert_body(w, E // 4 * r + i, E * r + 4 * i + w + 1, (E + 1) * r + 4 * i + w + 1)
                    last_rows(E * r + E)
            add_rows().then_inc(s_sum, 1)

        @block.scalar
        def _(act):
            act.nop().then_inc(s_evac, 2)
            act.nop().then_inc(s_ysb, FREE)

            def sumsq_std(k, src):
                for tt in range(TT):
                    nc.scalar.activation(normed[:, tt, :], src(tt), ACT.Square,
                                         accum_out=sumsq[:, tt:tt + 1]).then_inc(s_sq, 1)
                act.wait_ge(s_var, k + 1)
                nc.scalar.activation(std, var, ACT.Sqrt).then_inc(s_std, 1)

            def copy_unit(n, dst, src):
                act.wait_ge(s_unit, 2 + n)
                nc.scalar.copy(dst, src).then_inc(s_evac, 1)

            two = "p (a t) -> p a t"
            def evac_a(g, n):
                act.wait_ge(s_unit, 2 + 6 * g + n + 1)
                if n < 4:
                    dst = qk[:, n // 2, bass.ds(g, 1), 2 * (n % 2):2 * (n % 2) + 2, :]
                    src = bank(n % 2).rearrange("p (g a t) -> p g a t", g=1, a=2)
                else:
                    dst = v[:, bass.ds(g, 1), :, (n - 4) * 256:(n - 3) * 256]
                    src = bank(n % 2).rearrange("p (g a n) -> p g a n", g=1, a=2)
                nc.scalar.copy(dst, src).then_inc(s_evac, 1)

            act.wait_ge(s_x, 16)
            sumsq_std(0, lambda tt: h[:, tt, :])
            for tt in range(TT):
                act.wait_ge(s_xT, tt + 1)
                nc.scalar.copy(xT_hi[:, :, tt * P:(tt + 1) * P], x_whole[:, :, tt * P:(tt + 1) * P]).then_inc(s_xhi, 1)

            def high(k, src):
                for half in range(2):
                    cs = slice(4 * half, 4 * half + 4)
                    nc.scalar.copy(cut[:, k, 0, cs, :], src[:, cs, :]).then_inc(s_hi, 1)

            act.wait_ge(s_land[0], 16)
            high(0, land[0])
            with act.Fori(0, GROUPS) as g:
                for n in range(6):
                    act.wait_ge(s_land[(n + 1) % 6], 16 * g + 16 * (1 + (n + 1) // 6))
                    act.wait_ge(s_unit, 2 + 6 * g + n)
                    high((n + 1) % 2, land[(n + 1) % 6])
                    evac_a(g, n)
            def exps(i, u):
                act.wait_ge(s_nmax, 2 * i + u + 1)
                for tt, cs in ((0, slice(KEYS1, SCORES)), (1, slice(0, KEYS1))):
                    nc.scalar.activation(prob[:, cs], prob[:, cs], ACT.Exp, bias=nmax[:, u, tt:tt + 1],
                                         scale=HD ** -0.5, accum_out=psum_[:, u, tt:tt + 1]).then_inc(s_prob, 1)

            def copy_probs(i, u):
                act.wait_ge(s_ptp, 2 * i + u + 1)
                nc.scalar.copy(probT[:, :, :], ps[:, 5 * 512:5 * 512 + SCORES].rearrange("p (b q) -> p b q", q=P))\
                    .then_inc(s_pt, 1)

            def high_b(i, n, k):
                act.wait_ge(s_land[n % 5], 16 * i + 16 * (GROUPS + 1 + n // 5))
                act.wait_ge(s_unit, 2 + UNITS_A + 5 * i + n - 1)
                high(k, land[n % 5])

            def gate(i, b, k):
                act.wait_ge(s_unit, 2 + UNITS_A + 5 * i + 4 + b)
                for j in range(2):
                    ins = nc.scalar.activation(gates[:, b, bass.ds(2 * i + j, 1), :],
                                               bank(k, j * T, T).rearrange("p (a t) -> p a t", a=1),
                                               ACT.Sigmoid, bias=vecs[:, bass.ds(V_BGATE + b * DC + j + 2 * i, 1)])
                ins.then_inc(s_evac, 1)

            with act.Fori(0, PAIRS // 2) as ii:
                for q in range(2):
                    i = 2 * ii + q
                    high_b(i, 1, 1 - q)
                    exps(i, 0)
                    high_b(i, 2, q)
                    copy_probs(i, 0)
                    act.wait_ge(s_conv, FREE + i)
                    copy_unit(UNITS_A + 5 * i + 1, gb_sb, bank(q).rearrange(two, a=2))
                    high_b(i, 3, 1 - q)
                    exps(i, 1)
                    copy_unit(UNITS_A + 5 * i + 2, gc_sb[:, :, :], bank(1 - q).rearrange(two, a=2))
                    high_b(i, 4, q)
                    copy_probs(i, 1)
                    if q == 0:
                        high_b(i, 5, 1)
                    else:
                        with act.If(ii < PAIRS // 2 - 1):
                            high_b(i, 5, 0)
                    gate(i, 0, 1 - q)
                    gate(i, 1, q)
            act.wait_ge(s_yat, 1)
            nc.scalar.copy(yaT, ps[:, 2 * 512:4 * 512].rearrange("p (j t) -> p j t", j=4)).then_inc(s_yaT, 1)
            act.wait_ge(s_mem, 16)
            sumsq_std(1, lambda tt: mem_in[:, tt, :])
            act.wait_ge(s_h, 2 * TT)
            act.wait_ge(s_trn, 2 * TT)
            sumsq_std(2, lambda tt: h[:, tt, :])
            for j in range(2):
                copy_unit(UNITS_B + 1 + j, kmT[:, 2 * j:2 * j + 2, :], bank(j).rearrange(two, a=2))
            for tt in range(TT):
                copy_unit(UNITS_B + 3 + tt, vm[:, tt, :], bank(tt))
            for j in range(2):
                copy_unit(UNITS_M + 1 + j, qcT[:, 2 * j:2 * j + 2, :], bank(j).rearrange(two, a=2))
            for tt in range(TT):
                act.wait_ge(s_cm, tt + 1)
                for m in range(MH):
                    nc.scalar.activation(pc[:, tt, m, :], bank(2 + 2 * tt, m * T, T), ACT.Exp,
                                         bias=cneg[:, tt, m:m + 1], scale=MHD ** -0.5,
                                         accum_out=csum[:, tt, m:m + 1]).then_inc(s_ce, 1)
            for tt in range(TT):
                act.wait_ge(s_ct, tt + 1)
                nc.scalar.copy(pcT[:, tt, :, :, :], bank((6, 2)[tt], 0, 1024)
                               .rearrange("p (m b t) -> p m b t", m=MH, b=TT)).then_inc(s_cpt, 1)
                act.wait_ge(s_cv, tt + 1)
                nc.scalar.copy(ocT[:, tt, :, :], bank(tt).rearrange("p (m t) -> p m t", m=MH)).then_inc(s_co_t, 1)
            act.wait_ge(s_h, 4 * TT)
            sumsq_std(3, lambda tt: h[:, tt, :])
            act.dma_start(g_fin, io["norm_final"].rearrange("(a d) -> a d", a=1).to_broadcast([P, D])).then_inc(s_gfin, 16)
            act.wait_ge(s_top, 1)
            for tt in range(TT):
                nc.scalar.activation(gate_w[:, tt, :], logit[:, tt, 0:E], ACT.Exp,
                                     bias=topneg[:, tt:tt + 1]).then_inc(s_ex, 1)
            act.wait_ge(s_sprt, 1)
            nc.scalar.copy(spreadT, bank(4, 0, TT * P).rearrange("p (a t) -> p a t", a=TT)).then_inc(s_sprT, 1)

            def expert_body(count):
                act.wait_ge(s_g, count)
                nc.scalar.activation(act_s, act_g, ACT.Sigmoid, scale=ALPHA).then_inc(s_sig, 1)
                act.wait_ge(s_ht, count)
                nc.scalar.copy(hdnT, bank(6).rearrange("p (j s) -> p j s", j=4)).then_inc(s_hT, 1)
                act.wait_ge(s_sprt, FREE + count)
                nc.scalar.copy(spreadT, bank(4, 0, TT * P).rearrange("p (a t) -> p a t", a=TT)).then_inc(s_sprT, 1)
                act.wait_ge(s_y, count)
                nc.scalar.copy(y_sb, bank(7)).then_inc(s_ysb, 1)

            with act.Fori(0, E // 2) as i:
                for u in range(2):
                    expert_body(2 * i + u + 1)
            act.wait_ge(s_rounds, 1)
            rounds = act.value_load(rounds_i[0:1, 0:1], min_val=1, max_val=T // SLOTS)
            with act.If(rounds > 1):
                with act.Fori(1, rounds) as r:
                    with act.Fori(0, E // 2) as i:
                        for u in range(2):
                            expert_body(E * r + 2 * i + u + 1)
            act.wait_ge(s_sum, 1)
            sumsq_std(4, lambda tt: bank(2 * tt, 0, D))

        @block.vector
        def _(dve):
            steps = [0]

            def link(ins):
                steps[0] += 1
                ins.then_inc(s_dve, 1)
                dve.wait_ge(s_dve, steps[0])

            def norm(k, src, permuted=False):
                dve.wait_ge(s_sq, TT * (k + 1))
                nc.vector.tensor_scalar(var, sumsq, 1.0 / D, EPS, ALU.mult, ALU.add).then_inc(s_var, 1)
                dve.wait_ge(s_std, k + 1)
                link(nc.vector.reciprocal(rstd, std))
                for tt in range(TT):
                    dst, x = normed[:, tt, :], src(tt)
                    if permuted:
                        dst = dst.rearrange("t (c p) -> t c p", c=DC)
                        x = x.rearrange("t (p c) -> t c p", c=DC)
                    nc.vector.tensor_scalar(dst, x, rstd[:, tt:tt + 1], None, ALU.mult).then_inc(s_nrm, 1)

            def gained(k, dst, gain):
                for tt in range(TT):
                    dve.wait_ge(s_trn, TT * k + tt + 1)
                    nc.vector.tensor_tensor(dst[:, :, tt * P:(tt + 1) * P],
                                            bank(4 + 2 * tt, 0, D).rearrange("p (c t) -> p c t", c=DC),
                                            gain.rearrange("p (c o) -> p c o", o=1).to_broadcast([P, DC, P]),
                                            ALU.mult).then_inc(s_xT, 1)

            dve.nop().then_inc(s_scread, FREE)
            dve.nop().then_inc(s_ya, FREE)
            dve.nop().then_inc(s_conv, FREE)
            dve.wait_ge(s_vecT, 1)
            link(nc.vector.tensor_copy(vecs[:, :], bank(2, 0, V_ALL)))
            norm(0, lambda tt: h[:, tt, :])
            gained(0, x_whole, vecs[:, V_MIX:V_MIX + DC])
            for tt in range(TT):
                ts = slice(tt * P, (tt + 1) * P)
                dve.wait_ge(s_xhi, tt + 1)
                nc.vector.tensor_tensor(xT_lo[:, :, ts], x_whole[:, :, ts], xT_hi[:, :, ts].bitcast(F32), ALU.subtract)\
                    .then_inc(s_xlo, 1)

            def low(k, src, m):
                for half in range(2):
                    cs = slice(4 * half, 4 * half + 4)
                    dve.wait_ge(s_hi, 2 * m + half + 1)
                    nc.vector.tensor_tensor(cut[:, k, 1, cs, :], src[:, cs, :], cut[:, k, 0, cs, :].bitcast(F32),
                                            ALU.subtract).then_inc(s_lo, 1)

            low(0, land[0], 0)
            with dve.Fori(0, GROUPS) as g:
                for n in range(6):
                    low((n + 1) % 2, land[(n + 1) % 6], 6 * g + n + 1)

            def soft(i, u, n):
                dve.wait_ge(s_score, 2 + 2 * i + u + 1)
                slope = const[:, bass.ds(C_SLOPE + u + 2 * i, 1)]
                for cs, b in ((slice(0, KEYS1), 2), (slice(KEYS1, SCORES), 4)):
                    ins = nc.vector.scalar_tensor_tensor(
                        out=prob[:, cs], in0=const[:, C_DIST + cs.start:C_DIST + cs.stop], scalar=slope,
                        in1=bank(b, 0, cs.stop - cs.start), op0=ALU.mult, op1=ALU.add)
                ins.then_inc(s_scread, 1)
                dve.wait_ge(s_scread, FREE + 2 * i + u + 1)
                for tt, cs in ((0, slice(KEYS1, SCORES)), (1, slice(0, KEYS1))):
                    ins = nc.vector.tensor_reduce(rowmax[:, tt:tt + 1], prob[:, cs], AX_X, ALU.max)
                n(ins)
                nc.vector.tensor_scalar(nmax[:, u, :], rowmax, -HD ** -0.5, None, ALU.mult).then_inc(s_nmax, 1)

            def take_out(i, u, n):
                dve.wait_ge(s_prob, 2 * (2 * i + u) + 2)
                n(nc.vector.reciprocal(rinv[:, u, :], psum_[:, u, :]))
                dve.wait_ge(s_pv, 2 * i + u + 1)
                for tt in range(TT):
                    ins = nc.vector.tensor_scalar(ya[:, tt, bass.ds(2 * HD * i + u * HD, HD)],
                                                  bank(7, 256 + tt * HD, HD), rinv[:, u, tt:tt + 1], None, ALU.mult)
                ins.then_inc(s_ya, 1)

            dve.wait_ge(s_const, 16)
            dve.wait_ge(s_zero, 5)
            base, per = steps[0], 7
            with dve.Fori(0, PAIRS // 2) as ii:
                for q in range(2):
                    i = 2 * ii + q
                    k = [0]

                    def n(ins):
                        k[0] += 1
                        ins.then_inc(s_dve, 1)
                        dve.wait_ge(s_dve, base + per * i + k[0])

                    soft(i, 0, n)
                    low(1 - q, land[1], UNITS_A + 5 * i + 1)
                    low(q, land[2], UNITS_A + 5 * i + 2)
                    soft(i, 1, n)
                    take_out(i, 0, n)
                    low(1 - q, land[3], UNITS_A + 5 * i + 3)
                    dve.wait_ge(s_unit, 2 + UNITS_A + 5 * i + 3)
                    dve.wait_ge(s_evac, 2 + UNITS_A + 4 * i + 2)
                    nc.vector.tensor_tensor(conv_z[:, :, CONV_K - 1:], bank(q).rearrange("p (a t) -> p a t", a=2),
                                            gc_sb[:, :, :], ALU.mult).then_inc(s_xc, 1)
                    low(q, land[4], UNITS_A + 5 * i + 4)
                    dve.wait_ge(s_xc, i + 1)
                    for tap in range(CONV_K):
                        for j in range(2):
                            w = vecs[:, bass.ds(V_CONV + tap * DC + j + 2 * i, 1)]
                            z = conv_z[:, j:j + 1, tap:tap + T]
                            y = ycT[:, bass.ds(2 * i + j, 1), :]
                            if tap == 0:
                                ins = nc.vector.tensor_scalar(y, z, w, None, ALU.mult)
                            else:
                                ins = nc.vector.scalar_tensor_tensor(out=y, in0=z, scalar=w, in1=y,
                                                                     op0=ALU.mult, op1=ALU.add)
                        n(ins)
                    nc.vector.tensor_tensor(ycT[:, bass.ds(2 * i, 2), :], ycT[:, bass.ds(2 * i, 2), :], gb_sb, ALU.mult)\
                        .then_inc(s_conv, 1)
                    take_out(i, 1, n)
                    assert k[0] == per
                    if q == 0:
                        low(1, land[0], UNITS_A + 5 * i + 5)
                    else:
                        with dve.If(ii < PAIRS // 2 - 1):
                            low(0, land[0], UNITS_A + 5 * i + 5)
            steps[0] += per * PAIRS

            for m in range(DC):
                dve.wait_ge(s_mixp, m + 1)
                nc.vector.tensor_tensor(mix_a[:, m % 2, :], bank(m % 2, 0, T), gates[:, 0, m, :], ALU.mult)
                nc.vector.tensor_tensor(mix_b[:, m % 2, :], bank(m % 2, T, T), gates[:, 1, m, :], ALU.mult)\
                    .then_inc(s_mixread, 1)
                dve.wait_ge(s_mixread, m + 1)
                nc.vector.tensor_tensor(mixT[:, m, :], mix_a[:, m % 2, :], mix_b[:, m % 2, :], ALU.add)\
                    .then_inc(s_mix, 1)
                if m == 3:
                    norm(1, lambda tt: mem_in[:, tt, :])
            gained(1, memT, vecs[:, V_MEM:V_MEM + DC])
            for half in range(2):
                for tt in range(TT):
                    dve.wait_ge(s_hp, 2 * half + tt + 1)
                    hh = h[:, tt, half * 512:(half + 1) * 512]
                    nc.vector.tensor_tensor(hh, bank(2 + 2 * half + tt), hh, ALU.add).then_inc(s_h, 1)
            dve.wait_ge(s_h, 2 * TT)
            norm(2, lambda tt: h[:, tt, :])
            gained(2, xT, vecs[:, V_CROSS:V_CROSS + DC])
            for tt in range(TT):
                dve.wait_ge(s_cs, tt + 1)
                link(nc.vector.tensor_reduce(cmax[:, tt, :], bank(2 + 2 * tt, 0, MH * T)
                                             .rearrange("p (m k) -> p m k", m=MH), AX_X, ALU.max))
                nc.vector.tensor_scalar(cneg[:, tt, :], cmax[:, tt, :], -MHD ** -0.5, None, ALU.mult).then_inc(s_cm, 1)
            for tt in range(TT):
                dve.wait_ge(s_ce, MH * (tt + 1))
                link(nc.vector.reciprocal(cinv[:, tt, :], csum[:, tt, :]))
                nc.vector.tensor_tensor(pc[:, tt, :, :], pc[:, tt, :, :],
                                        cinv[:, tt, :].rearrange("p (m o) -> p m o", o=1).to_broadcast([P, MH, T]),
                                        ALU.mult).then_inc(s_cn, 1)
            for tt in range(TT):
                for half in range(2):
                    dve.wait_ge(s_hp, 2 * TT + 2 * tt + half + 1)
                    hh = h[:, tt, half * 512:(half + 1) * 512]
                    nc.vector.tensor_tensor(hh, bank(4 + 2 * tt + half), hh, ALU.add).then_inc(s_h, 1)
            dve.wait_ge(s_h, 4 * TT)
            norm(3, lambda tt: h[:, tt, :], permuted=True)
            dve.wait_ge(s_wr, 48)
            gained(3, xT, g_moe[:, :])
            dve.wait_ge(s_lg, 1)
            for tt in range(TT):
                ins = nc.vector.tensor_tensor(logit[:, tt, 0:E], bank(6, tt * E, E), rb[:, :], ALU.add)
            link(ins)
            for tt in range(TT):
                ins = nc.vector.max(top8[:, tt, :], logit[:, tt, 0:E])
            link(ins)
            nc.vector.tensor_scalar(topneg, top8[:, :, 0], -1.0, None, ALU.mult).then_inc(s_top, 1)
            link(nc.vector.tensor_copy(wanted[:, :, 0:TOPK], top8[:, :, 0:TOPK]))
            for tt in range(TT):
                ins = nc.vector.match_replace(out=logit_r[:, tt, :], in_to_replace=wanted[:, tt, :],
                                              in_values=logit[:, tt, :], imm_value=TAKEN)
            link(ins)
            for tt in range(TT):
                nc.vector.tensor_tensor(chosen[:, tt, :], logit_r[:, tt, 0:E], logit[:, tt, 0:E], ALU.is_lt)\
                    .then_inc(s_sel, 1)
            dve.wait_ge(s_sel, TT)
            dve.wait_ge(s_ex, TT)
            link(nc.vector.tensor_tensor(gate_w[:, :, :], gate_w[:, :, :], chosen[:, :, :], ALU.mult))
            link(nc.vector.tensor_reduce(topsum, gate_w[:, :, :], AX_X, ALU.add))
            link(nc.vector.reciprocal(topinv, topsum))
            for tt in range(TT):
                ins = nc.vector.tensor_scalar(gate_w[:, tt, :], gate_w[:, tt, :], topinv[:, tt:tt + 1], None, ALU.mult)
            link(ins)
            dve.wait_ge(s_zero, 9)
            for half in range(2):
                ins = nc.vector.tensor_copy(spread[:, :, half * SLOTS:half * SLOTS + E], gate_w[:, :, :])
            ins.then_inc(s_w, 1)
            dve.wait_ge(s_w, 1)
            dve.wait_ge(s_pos, 1)
            for tt in range(TT):
                ins = nc.vector.scalar_tensor_tensor(out=place[:, tt, 0:E], in0=bank(7, tt * E, E), scalar=1.0,
                                                     in1=chosen[:, tt, :], op0=ALU.add, op1=ALU.mult)
            link(ins)
            link(nc.vector.tensor_scalar(place[:, :, 0:E], place[:, :, 0:E], -1.0, None, ALU.add))
            link(nc.vector.tensor_reduce(most, bank(7, 2 * E, E), AX_X, ALU.max))
            link(nc.vector.tensor_scalar(rounds_f[:, 0:1], most, float(SLOTS), 1.0, ALU.is_gt, ALU.add))
            for k in range(2):
                link(nc.vector.scalar_tensor_tensor(out=rounds_f[:, k + 1:k + 2], in0=most, scalar=float(SLOTS * (k + 2)),
                                                    in1=rounds_f[:, k:k + 1], op0=ALU.is_gt, op1=ALU.add))
            nc.vector.tensor_copy(rounds_i[:, :], rounds_f[:, 2:3]).then_inc(s_rounds, 1)

            slots1, slots2 = const[:, C_SLOT:C_SLOT + SLOTS], const[:, C_SLOT:C_SLOT + 2 * SLOTS]

            def picks(e):
                for tt in range(TT):
                    nc.vector.tensor_scalar(pick[:, tt, :], slots1, place[:, tt, bass.ds(e, 1)], None, ALU.is_equal)\
                        .then_inc(s_pick, 1)

            def spreads(e):
                for tt in range(TT):
                    nc.vector.tensor_scalar(spread[:, tt, :], slots2, place[:, tt, bass.ds(e, 1)],
                                            gate_w[:, tt, bass.ds(e, 1)], ALU.is_equal, ALU.mult).then_inc(s_spr, 1)

            def take_gathered(gathers):
                dve.wait_ge(s_gat, gathers)
                nc.vector.tensor_tensor(xg[:, :, :], bank(6).rearrange("p (c s) -> p c s", c=DC),
                                        g_moe[:, :].rearrange("p (c o) -> p c o", o=1).to_broadcast([P, DC, SLOTS]),
                                        ALU.mult).then_inc(s_xg, 1)

            def expert_body(e, count, gathers):
                picks(e + 1)
                dve.wait_ge(s_sprt, count)
                spreads(e)
                dve.wait_ge(s_gate, count)
                nc.vector.tensor_scalar(act_g, bank(4), LIMIT, None, ALU.min).then_inc(s_g, 1)
                dve.wait_ge(s_sig, count)
                nc.vector.tensor_tensor(act_s, act_g, act_s, ALU.mult)
                dve.wait_ge(s_up, count)
                ins = nc.vector.tensor_scalar(act_l, bank(5), -LIMIT, LIMIT, ALU.max, ALU.min)
                ins.then_inc(s_lin, 1)
                dve.wait_ge(s_lin, count)
                nc.vector.scalar_tensor_tensor(out=hdn, in0=act_l, scalar=1.0, in1=act_s, op0=ALU.add, op1=ALU.mult)\
                    .then_inc(s_hdn, 1)
                take_gathered(gathers + 1)

            dve.wait_ge(s_rounds, 1)
            picks(0)
            take_gathered(1)
            with dve.Fori(0, E // 2) as i:
                for u in range(2):
                    expert_body(2 * i + u, 2 * i + u + 1, 2 * i + u + 1)
            rounds = dve.value_load(rounds_i[0:1, 0:1], min_val=1, max_val=T // SLOTS)
            with dve.If(rounds > 1):
                with dve.Fori(1, rounds) as r:
                    nc.vector.tensor_scalar(place[:, :, :], place[:, :, :], -float(SLOTS), None, ALU.add)\
                        .then_inc(s_route, 1)
                    dve.wait_ge(s_route, r)
                    picks(0)
                    take_gathered((E + 1) * r + 1)
                    with dve.Fori(0, E // 2) as i:
                        for u in range(2):
                            expert_body(2 * i + u, E * r + 2 * i + u + 1, (E + 1) * r + 2 * i + u + 1)
            dve.wait_ge(s_sq, TT * 5)
            nc.vector.tensor_scalar(var, sumsq, 1.0 / D, EPS, ALU.mult, ALU.add).then_inc(s_var, 1)
            dve.wait_ge(s_std, 5)
            link(nc.vector.reciprocal(rstd, std))
            dve.wait_ge(s_gfin, 16)
            for tt in range(TT):
                nc.vector.scalar_tensor_tensor(out=outp[:, tt, :], in0=bank(2 * tt, 0, D), scalar=rstd[:, tt:tt + 1],
                                               in1=g_fin, op0=ALU.mult, op1=ALU.mult).then_inc(s_out, 1)


_IN = ("x", "mem", "norm_mix", "w_in", "conv_w", "w_branch_attn", "w_branch_conv", "w_gate", "b_gate", "w_out",
       "norm_cross", "norm_mem", "w_cq", "w_ckv", "w_co", "norm_moe", "router_w", "router_b",
       "w_exp_gate", "b_exp_gate", "w_exp_up", "b_exp_up", "w_exp_down", "b_exp_down", "norm_final")


def kernel(**inputs):
    import concourse.bacc as bacc
    from concourse.bass_utils import run_bass_kernel_spmd

    nc = bacc.Bacc("TRN2", target_bir_lowering=False, num_devices=1)
    arrays, io = {}, {}
    for name in _IN:
        a = np.ascontiguousarray(inputs[name])
        if name != "norm_final":
            a = a.reshape(a.shape[1:])
        if name == "conv_w":
            a = a.reshape(-1)
        arrays[f"in_{name}"] = a
    arrays["in_const"] = constants()
    for key, a in arrays.items():
        io[key[3:]] = nc.dram_tensor(key, a.shape, F32, kind="ExternalInput").ap()
    io["out"] = nc.dram_tensor("out_h", (T, D), F32, kind="ExternalOutput").ap()
    build(nc, io)
    r = run_bass_kernel_spmd(nc, [arrays], core_ids=[0])
    return r.results[0]["out_h"].reshape(inputs["x"].shape)
```

```python
from contextlib import ExitStack

import numpy as np

import concourse.bass as bass
from concourse import mybir

F32 = mybir.dt.float32
F32R = mybir.dt.float32r
I32 = mybir.dt.int32
ALU = mybir.AluOpType
ACT = mybir.ActivationFunctionType
AX_X = mybir.AxisListType.X

P = 128
T, D = 256, 1024
TT = T // P
DC = D // P
GROUPS, HEADS, HD = 3, 8, 64
AW = HEADS * HD
DILATION = (1, 4, 16)
WINDOW_STEPS = 128
PAIRS = HEADS // 2
CONV_K = 3
MH, MHD = 4, 128
E, TOPK, FF = 32, 4, 1024
SLOTS = 64
LIMIT, ALPHA, EPS = 7.0, 1.702, 1e-6
SENTINEL, TAKEN = -3.0e38, -3.3e38
MASKED = 1e30

KEYS1, KEYS0 = GROUPS * T, GROUPS * P
SCORES = KEYS1 + KEYS0
BLOCKS = SCORES // P

C_IDENT = 0
C_DIST = C_IDENT + P
C_BEFORE = C_DIST + SCORES
C_ONES = C_BEFORE + P
C_SLOT = C_ONES + P
C_PICK = C_SLOT + 2 * SLOTS
C_SLOPE = C_PICK + 3 * SLOTS
C_ALL = C_SLOPE + HEADS

V_MEM, V_MIX, V_CROSS = 0, DC, 2 * DC
V_BGATE = 3 * DC
V_CONV = V_BGATE + 2 * DC
V_ALL = V_CONV + CONV_K * DC


def constants():
    c = np.zeros((P, C_ALL), np.float32)
    c[:, C_IDENT:C_IDENT + P] = np.eye(P)
    q, k = np.arange(T)[:, None], np.arange(T)[None, :]
    for g, dil in enumerate(DILATION):
        d = q - k
        ok = (d >= 0) & (d % dil == 0) & (d <= WINDOW_STEPS * dil)
        dist = np.where(ok, d, MASKED).astype(np.float32)
        c[:, C_DIST + g * T:C_DIST + (g + 1) * T] = dist[P:, :]
        c[:, C_DIST + KEYS1 + g * P:C_DIST + KEYS1 + (g + 1) * P] = dist[:P, :P]
    c[:, C_BEFORE:C_BEFORE + P] = np.arange(P)[:, None] < np.arange(P)[None, :]
    c[:, C_ONES:C_ONES + P] = 1.0
    c[:, C_SLOT:C_SLOT + 2 * SLOTS] = np.tile(np.arange(SLOTS), 2)[None, :]
    for r in range(3):
        c[r, C_PICK + r * SLOTS:C_PICK + (r + 1) * SLOTS] = 1.0
    c[:, C_SLOPE:C_SLOPE + HEADS] = -(2.0 ** -np.arange(1.0, HEADS + 1)) * HD ** 0.5
    return c


def build(nc, io):
    ctx = ExitStack()
    with ctx:
        def sb(name, shape, dt=F32):
            return ctx.enter_context(nc.sbuf_tensor(name, shape, dt))

        def sem(name):
            return ctx.enter_context(nc.semaphore(name))

        SLOT_N = DC * 512
        ring = sb("ring", [P, 6 * SLOT_N])
        ring_at = nc.sbuf_base - 6 * SLOT_N * 4

        def slot(s):
            return ring[:, s * SLOT_N:(s + 1) * SLOT_N]

        const = sb("const", [P, C_ALL])
        ident = const[:, C_IDENT:C_IDENT + P]
        h = sb("h", [P, TT, D])
        xT = sb("xT", [P, DC, T])
        xT_at = nc.sbuf_base - DC * T * 4
        ycT = sb("ycT", [P, DC, T])
        qk = sb("qk", [P, 2, GROUPS, PAIRS, T])
        qk_at = nc.sbuf_base - 2 * GROUPS * PAIRS * T * 4
        v = sb("v", [P, GROUPS, TT, AW])
        gates = sb("gates", [P, 2, DC, T])
        gates_at = nc.sbuf_base - 2 * DC * T * 4
        kmT = sb("kmT", [P, MH, T])
        vm = sb("vm", [P, TT, MH * MHD])
        prob = sb("prob", [P, SCORES])
        probT = sb("probT", [P, BLOCKS, P])
        ya = sb("ya", [P, TT, AW])
        vecs = sb("vecs", [P, V_ALL])
        small = sb("small", [P, 64])
        warm = sb("warm", [P, 2])
        wr = sb("wr", [P, DC, E])
        rb = sb("rb", [P, E])
        g_moe = sb("g_moe", [P, DC])
        rounds_i = sb("rounds_i", [P, 1], I32)

        mem_in = v[:, :, :, :].rearrange("p g a n -> p (g a n)")[:, 0:TT * D].rearrange("p (a d) -> p a d", a=TT)
        flat_qk = qk[:, :, :, :, :].rearrange("p u g a t -> p (u g a t)")
        normed = flat_qk[:, 0:TT * D].rearrange("p (a d) -> p a d", a=TT)
        vec_rows = prob[0:V_ALL, 0:P]
        PIECE_N = DC * 256
        land = [ring[:, n * PIECE_N:(n + 1) * PIECE_N].rearrange("p (c n) -> p c n", c=DC) for n in range(6)]
        cut = nc.alloc_sbuf_tensor_at("cut", [P, 2, 2, DC, 256], F32R, offset=ring_at + 3 * SLOT_N * 4)
        xT_hi = nc.alloc_sbuf_tensor_at("xT_hi", [P, DC, T], F32R, offset=xT_at)
        xT_lo = nc.alloc_sbuf_tensor_at("xT_lo", [P, DC, T], F32R, offset=ring_at + 5 * SLOT_N * 4 + 2048 * 4)
        x_part = (xT_hi, xT_lo)
        spare = ring[:, 5 * SLOT_N:5 * SLOT_N + 2048]
        x_whole = gates[:, :, :, :].rearrange("p a c t -> p (a c t)")[:, 0:DC * T].rearrange("p (c t) -> p c t", c=DC)
        stage_q = spare[:, 0:2 * GROUPS * T].rearrange("p (u g t) -> p u g t", u=2, g=GROUPS)
        gb_sb = spare[:, 2 * GROUPS * T:2 * GROUPS * T + 2 * T].rearrange("p (a t) -> p a t", a=2)
        gc_sb = sb("gc_sb", [P, 2, T])
        conv_z = sb("conv_z", [P, 2, T + CONV_K - 1])
        mixT = flat_qk[:, TT * D:TT * D + DC * T].rearrange("p (c t) -> p c t", c=DC)
        mix_b = conv_z[:, :, 0:T]
        memT = ring[:, 5 * SLOT_N + 2048:6 * SLOT_N].rearrange("p (c t) -> p c t", c=DC)

        def parts_at(name, chunks, hi_at, lo_at):
            return [nc.alloc_sbuf_tensor_at(f"{name}_{part}", [P, chunks, T], F32R, offset=at)
                    for part, at in (("hi", hi_at), ("lo", lo_at))]

        ya_part = parts_at("ya", 4, qk_at + (TT * D + DC * T) * 4, qk_at + (TT * D + (DC + 4) * T) * 4)
        yc_part = parts_at("yc", DC, xT_at, xT_at + DC * T * 4)
        mix_part = parts_at("mix", DC, ring_at + 5 * SLOT_N * 4, qk_at + TT * D * 4)
        mem_part = parts_at("memT", DC, gates_at, ring_at + (5 * SLOT_N + 2048) * 4)
        x2_part = parts_at("x2", DC, xT_at, xT_at + DC * T * 4)
        x2 = ycT[:, :, :]
        flat_v = v[:, :, :, :].rearrange("p g a n -> p (g a n)")
        qcT = flat_v[:, 0:MH * T].rearrange("p (m t) -> p m t", m=MH)
        ocT = flat_v[:, MH * T:2 * MH * T].rearrange("p (a m t) -> p a m t", a=TT, m=MH)
        flat_g = gates[:, :, :, :].rearrange("p a c t -> p (a c t)")
        pc = flat_g[:, 0:TT * MH * T].rearrange("p (a m k) -> p a m k", a=TT, m=MH)
        pcT = flat_g[:, TT * MH * T:2 * TT * MH * T].rearrange("p (a m b t) -> p a m b t", a=TT, m=MH, b=TT)

        logit = sb("logit", [P, TT, E + 4])
        top8 = sb("top8", [P, TT, 8])
        wanted = sb("wanted", [P, TT, 8])
        flat_pt = probT[:, :, :].rearrange("p b q -> p (b q)")
        logit_r = flat_pt[:, 0:TT * (E + 4)].rearrange("p (a e) -> p a e", a=TT)
        chosen = flat_pt[:, 128:128 + TT * E].rearrange("p (a e) -> p a e", a=TT)
        gate_w = flat_pt[:, 256:256 + TT * E].rearrange("p (a e) -> p a e", a=TT)
        place = sb("place", [P, TT, E + 2])
        f = 0

        def region(n):
            nonlocal f
            f += n
            assert f <= 2 * DC * T
            return flat_g[:, f - n:f]

        act_g = region(512)
        act_s = region(512)
        act_l = region(512)
        hdn = region(512)
        hdnT = region(512).rearrange("p (j s) -> p j s", j=4)
        y_sb = region(512)
        spread = region(2 * P).rearrange("p (a s) -> p a s", a=TT)
        spreadT = region(2 * P).rearrange("p (a t) -> p a t", a=TT)
        xg = prob[:, 0:DC * SLOTS].rearrange("p (c s) -> p c s", c=DC)
        pick = prob[:, DC * SLOTS:DC * SLOTS + TT * SLOTS].rearrange("p (a s) -> p a s", a=TT)
        bias = [flat_v[:, u * D:(u + 1) * D] for u in range(2)]
        more_slots = (flat_qk[:, TT * D:TT * D + SLOT_N],
                      nc.alloc_sbuf_tensor_at("slot7", [P, SLOT_N], F32, offset=xT_at)[:, :])
        outp = normed
        g_fin = flat_v[:, 2 * MH * T:2 * MH * T + D]

        ps = ctx.enter_context(nc.psum_tensor("ps", [P, 8 * 512], F32))

        def bank(b, lo=0, n=512):
            return ps[:, b * 512 + lo:b * 512 + lo + n]

        sumsq, var, std, rstd = (small[:, 2 * k:2 * k + 2] for k in range(4))
        nmax = small[:, 8:12].rearrange("p (u a) -> p u a", u=2)
        psum_ = small[:, 12:16].rearrange("p (u a) -> p u a", u=2)
        rinv = small[:, 16:20].rearrange("p (u a) -> p u a", u=2)
        rowmax = small[:, 20:22]
        cmax, cneg, csum, cinv = (small[:, 22 + 8 * k:30 + 8 * k].rearrange("p (a m) -> p a m", a=TT)
                                  for k in range(4))
        topneg, topsum, topinv = (small[:, 54 + 2 * k:56 + 2 * k] for k in range(3))
        most = small[:, 60:61]
        rounds_f = small[:, 61:64]

        s_ident, s_const, s_vec, s_x, s_mem, s_wr, s_bd, s_gfin = (sem(n) for n in (
            "ident_loaded", "const_loaded", "vec_loaded", "x_loaded", "mem_loaded", "router_loaded", "down_bias_loaded", "final_gain_loaded"))
        s_land = [sem(f"piece_loaded{n}") for n in range(6)]
        s_hi, s_lo = sem("hi_parts_ready"), sem("lo_parts_ready")
        s_xhi, s_xlo = sem("x_hi_ready"), sem("x_lo_ready")
        s_co = sem("w_co_loaded")
        s_yahi, s_yalo, s_ychi, s_yclo, s_mixhi, s_mixlo, s_memhi, s_memlo, s_x2hi, s_x2lo = (sem(n) for n in (
            "ya_hi_ready", "ya_lo_ready", "yc_hi_ready", "yc_lo_ready", "mix_hi_ready", "mix_lo_ready",
            "mem_hi_ready", "mem_lo_ready", "x2_hi_ready", "x2_lo_ready"))
        s_slot = [sem(f"expert_part_loaded{n}") for n in range(8)]
        s_bias = [sem(f"bias_loaded{n}") for n in range(2)]
        s_half = sem("first_half_used")
        s_zero, s_warm = sem("zeros_written"), sem("warm_written")
        s_dve = sem("vector_step")
        s_table = sem("sqrt_table_loaded")
        s_vecT, s_vecs = sem("vec_turned"), sem("vec_ready")
        s_sq, s_var, s_std, s_nrm, s_trn, s_xT = (sem(n) for n in (
            "sumsq_ready", "var_ready", "std_ready", "normed_ready", "normed_turned", "xT_ready"))
        s_unit, s_evac = sem("projection_ready"), sem("projection_copied")
        s_stage, s_score, s_scread = sem("q_staged"), sem("scores_ready"), sem("scores_read")
        s_nmax, s_prob, s_ptp, s_pt = (sem(n) for n in (
            "max_ready", "prob_ready", "prob_turned", "probT_ready"))
        s_pv, s_ya = sem("attn_out_ready"), sem("ya_ready")
        s_xc, s_conv = sem("xc_used"), sem("conv_done")
        s_yat = sem("ya_turned")
        s_mixread, s_mix = sem("branch_read"), sem("mix_ready")
        s_hp, s_h = sem("h_addend_ready"), sem("h_ready")
        s_cs, s_cm, s_ce, s_cn, s_ct, s_cpt, s_cv, s_co_t = (sem(n) for n in (
            "cross_scores", "cross_max", "cross_exp", "cross_prob", "cross_turned", "cross_probT",
            "cross_out", "cross_outT"))
        s_w = sem("token_weights_ready")
        s_lg, s_top, s_ex, s_sel, s_pos, s_route = (sem(n) for n in (
            "logits_ready", "top_ready", "top_exp_ready", "chosen_ready", "positions_ready", "routes_ready"))
        s_rounds = sem("rounds_ready")
        s_pick, s_gat, s_xg = sem("pick_ready"), sem("gathered"), sem("xg_ready")
        s_gate, s_g, s_sig, s_up, s_lin, s_hdn = (sem(n) for n in (
            "gate_ready", "gate_clamped", "sigmoid_ready", "up_ready", "up_clamped", "hdn_ready"))
        s_spr, s_sprt, s_sprT = sem("spread_ready"), sem("spread_turned"), sem("spreadT_ready")
        s_ht, s_hT, s_y, s_ysb, s_sum = (sem(n) for n in (
            "hdn_turned", "hdnT_ready", "y_ready", "y_copied", "sum_updated"))
        s_out = sem("out_ready")
        s_store = sem("out_stored")

        FREE = 1
        UNITS_A = 6 * GROUPS
        UNITS_B = UNITS_A + 5 * PAIRS
        COPIED_B = 2 + UNITS_A + 4 * PAIRS
        U_ATTN = UNITS_B
        U_CONV = U_ATTN + 2
        U_OUT = U_CONV + 4
        U_CKV = U_OUT + 4
        U_CQ = U_CKV + 4
        UNITS_D = U_CQ + 2
        RING = (6, 5, 0, 1, 3, 4, 2, 7)

        def part_place(w, k, fours=0):
            n = 6 * w + k
            return RING[n % len(RING)], 3 * fours + n // len(RING) + 1


        w_in = io["w_in"].rearrange("(c p) n -> p c n", p=P)
        w_gate = io["w_gate"].rearrange("(c p) n -> p c n", p=P)
        w_in_q = io["w_in"].rearrange("(c p) (q n) -> q p c n", p=P, n=256)
        w_gate_q = io["w_gate"].rearrange("(c p) (q n) -> q p c n", p=P, n=256)
        CONV0 = GROUPS * 3 * AW

        def wide_piece(piece):
            return piece.rearrange("p c n -> p (c n)").rearrange("p (c n) -> p c n", c=4)

        def rows(s):
            return (slot(s) if s < 6 else more_slots[s - 6]).rearrange("p (c n) -> p c n", c=4)

        block = ctx.enter_context(nc.Block())

        def load_expert(sp, w, e, free):
            wg = io["w_exp_gate"][bass.ds(e, 1)].rearrange("e (p c) n -> p (e c) n", c=DC)
            wu = io["w_exp_up"][bass.ds(e, 1)].rearrange("e (p c) n -> p (e c) n", c=DC)
            wd = io["w_exp_down"][bass.ds(e, 1)].rearrange("e (b p j) n -> p b (e j) n", b=2, j=4)
            parts = [wg[:, 0:4, :], wg[:, 4:8, :], wu[:, 0:4, :], wu[:, 4:8, :], wd[:, 0, :, :], wd[:, 1, :, :]]
            for k in range(6):
                place_, _ = part_place(w, k)
                sp.wait_ge(*free[k])
                sp.dma_start(rows(place_), parts[k]).then_inc(s_slot[place_], 16)

        def eight_before(e):
            return ((s_half, 3 * e - 3), (s_y, e - 1), (s_half, 3 * e - 2), (s_gate, e),
                    (s_half, 3 * e - 1), (s_up, e))

        @block.sync
        def _(sp):
            sp.dma_start(h[:, :, :], io["x"].rearrange("(a p) d -> p a d", p=P)).then_inc(s_x, 16)
            sp.dma_start(ident, io["const"][:, 0:P]).then_inc(s_ident, 16)
            for row, name, n in ((V_MEM, "norm_mem", DC), (V_MIX, "norm_mix", DC), (V_CROSS, "norm_cross", DC),
                                 (V_BGATE, "b_gate", 2 * DC), (V_CONV, "conv_w", CONV_K * DC)):
                sp.dma_start(vec_rows[row:row + n, :], io[name].rearrange("(a n) -> a n", n=P)).then_inc(s_vec, 16)
            for n in range(6):
                sp.dma_start(land[n], w_in_q[n]).then_inc(s_land[n], 16)
            sp.dma_start(const[:, P:], io["const"][:, P:]).then_inc(s_const, 16)
            sp.dma_start(wr[:, :, :], io["router_w"].rearrange("(p c) e -> p c e", c=DC)).then_inc(s_wr, 16)
            sp.dma_start(rb[:, :], io["router_b"].rearrange("(a e) -> a e", a=1).to_broadcast([P, E])).then_inc(s_wr, 16)
            sp.dma_start(g_moe[:, :], io["norm_moe"].rearrange("(p c) -> p c", c=DC)).then_inc(s_wr, 16)
            with sp.Fori(0, GROUPS - 1) as g:
                for n in range(6):
                    sp.wait_ge(s_lo, 2 * (6 * g + n) + 2)
                    sp.dma_start(land[n], w_in_q[bass.ds(6 * g + 6 + n, 1)].rearrange("q p c n -> p (q c) n"))\
                        .then_inc(s_land[n], 16)

            def load_pieces(i, cut_before):
                for n in range(5):
                    src = w_in_q[bass.ds(CONV0 // 256 + 4 * n + i, 1)] if n < 3 else \
                        w_gate_q[bass.ds(4 * (n - 3) + i, 1)]
                    sp.wait_ge(s_lo, cut_before(n))
                    sp.dma_start(land[n], src.rearrange("q p c n -> p (q c) n")).then_inc(s_land[n], 16)

            load_pieces(0, lambda n: 2 * (6 * GROUPS - 6 + n) + 2)
            with sp.Fori(0, PAIRS - 1) as i:
                load_pieces(i + 1, lambda n: 2 * (6 * GROUPS + 5 * i + n) + 2)

            def load_tail(first, last):
                for m in range(first, last):
                    n = (m - UNITS_B) % 4
                    dst = land[n]
                    if m < U_CONV:
                        dst = wide_piece(dst)
                        src = io["w_branch_attn"].rearrange("(c p) n -> p c n", p=P)[:, :, (m - U_ATTN) * 512:(m - U_ATTN + 1) * 512]
                    else:
                        name, k = next((name, m - u) for name, u in (("w_cq", U_CQ), ("w_ckv", U_CKV), ("w_out", U_OUT),
                                                                      ("w_branch_conv", U_CONV)) if m >= u)
                        src = io[name].rearrange("(c p) n -> p c n", p=P)[:, :, k * 256:(k + 1) * 256]
                    sp.wait_ge(s_lo, 2 * (m - 5 if m < UNITS_B + 4 else m - 4) + 2)
                    sp.dma_start(dst, src).then_inc(s_land[n], 16)

            load_tail(UNITS_B, UNITS_B + 4)
            sp.wait_ge(s_unit, 2 + UNITS_B)
            sp.dma_start(mem_in, io["mem"].rearrange("(a p) d -> p a d", p=P)).then_inc(s_mem, 16)
            load_tail(UNITS_B + 4, UNITS_B + 6)
            sp.wait_ge(s_lo, 2 * UNITS_B)
            sp.dma_start(rows(2), io["w_co"].rearrange("(c p) n -> p c n", p=P)).then_inc(s_co, 16)
            load_tail(UNITS_B + 6, UNITS_D)
            first = ((s_unit, 2 + U_CKV), (s_unit, 2 + U_CQ), (s_lo, 2 * U_CQ), (s_lo, 2 * UNITS_D),
                     (s_unit, 2 + UNITS_D), (s_unit, 2 + UNITS_D), (s_hp, 2 * TT), (s_lg, 1))
            load_expert(sp, 0, 0, first[0:6])
            load_expert(sp, 1, 1, first[6:8] + eight_before(1)[2:])
            for w in range(2, 4):
                load_expert(sp, w, w, eight_before(w))
            with sp.Fori(1, E // 4) as i:
                for w in range(4):
                    load_expert(sp, w, 4 * i + w, eight_before(4 * i + w))
            sp.wait_ge(s_rounds, 1)
            rounds = sp.value_load(rounds_i[0:1, 0:1], min_val=1, max_val=T // SLOTS)
            with sp.If(rounds > 1):
                with sp.Fori(1, rounds) as r:
                    with sp.Fori(0, E // 4) as i:
                        for w in range(4):
                            load_expert(sp, w, 4 * i + w, eight_before(E * r + 4 * i + w))
            for tt in range(TT):
                sp.wait_ge(s_out, tt + 1)
                sp.dma_start(io["out"][tt * P:(tt + 1) * P, :], outp[:, tt, :]).then_inc(s_store, 16)
            sp.wait_ge(s_store, 16 * TT)

        @block.gpsimd
        def _(pool):
            nc.gpsimd.memset(warm[:, 0:1], 1.0).then_inc(s_warm, 1)
            nc.gpsimd.memset(stage_q, 0.0).then_inc(s_zero, 1)
            nc.gpsimd.memset(conv_z[:, :, 0:CONV_K - 1], 0.0).then_inc(s_zero, 1)
            nc.gpsimd.memset(logit[:, :, E:E + 4], SENTINEL).then_inc(s_zero, 1)
            nc.gpsimd.memset(wanted[:, :, 4:8], SENTINEL).then_inc(s_zero, 1)
            nc.gpsimd.memset(place[:, :, E:E + 2], -1.0).then_inc(s_zero, 1)
            pool.wait_ge(s_zero, 5)
            pool.wait_ge(s_evac, 2 + UNITS_A - 4)
            with pool.Fori(0, PAIRS) as i:
                for u in range(2):
                    rs = slice(u * HD, (u + 1) * HD)
                    pool.wait_ge(s_score, 2 * i + u + 1)
                    nc.gpsimd.tensor_copy(stage_q[rs, u, :, :], qk[rs, 0, :, bass.ds(i, 1), :]).then_inc(s_stage, 1)
                    pool.wait_ge(s_stage, 2 * i + u + 1)
            pool.wait_ge(s_hp, 2 * TT)
            for u in range(2):
                nc.gpsimd.memset(bias[u], 0.0).then_inc(s_zero, 1)
            nc.gpsimd.memset(y_sb, 0.0).then_inc(s_zero, 1)
            nc.gpsimd.memset(spread[:, :, :], 0.0).then_inc(s_zero, 1)
            pool.wait_ge(s_zero, 9)
            for half in range(2):
                pool.dma_start(y_sb[half * SLOTS:half * SLOTS + E, :],
                               io["b_exp_down"][:, half * 512:(half + 1) * 512]).then_inc(s_bd, 16)

            def load_bias(u, e):
                for k, name in enumerate(("b_exp_gate", "b_exp_up")):
                    pool.dma_start(bias[u][k:k + 1, :], io[name][bass.ds(e, 1), :]).then_inc(s_bias[u], 16)

            for u in range(2):
                load_bias(u, u)
            with pool.Fori(1, E // 2) as i:
                for u in range(2):
                    pool.wait_ge(s_up, 2 * i + u - 1)
                    load_bias(u, 2 * i + u)
            pool.wait_ge(s_rounds, 1)
            rounds = pool.value_load(rounds_i[0:1, 0:1], min_val=1, max_val=T // SLOTS)
            with pool.If(rounds > 1):
                with pool.Fori(1, rounds) as r:
                    with pool.Fori(0, E // 2) as i:
                        for u in range(2):
                            pool.wait_ge(s_up, E * r + 2 * i + u - 1)
                            load_bias(u, 2 * i + u)

        @block.tensor
        def _(pe):
            def turn_vectors():
                pe.wait_ge(s_ident, 16)
                pe.wait_ge(s_vec, 16 * 5)
                nc.tensor.transpose(bank(2, 0, V_ALL), vec_rows, ident[0:V_ALL, 0:V_ALL]).then_inc(s_vecT, 1)

            def turn_normed(k):
                for tt in range(TT):
                    pe.wait_ge(s_nrm, TT * k + tt + 1)
                    for c in range(DC):
                        last = nc.tensor.transpose(bank(4 + 2 * tt, c * P, P), normed[:, tt, c * P:(c + 1) * P], ident)
                    last.then_inc(s_trn, 1)

            pe.nop().then_inc(s_score, 2)
            pe.nop().then_inc(s_unit, 2)
            turn_vectors()
            turn_normed(0)
            PARTS = ((0, 0), (0, 1), (1, 0))
            HIGH, LOW = PARTS[:2], PARTS[2:]

            def project_cut(b, k, transposed, cut_before, x_part=x_part, wait_x=None):
                for j in range(2):
                    for half in range(2):
                        for ready, parts in ((s_hi, HIGH), (s_lo, LOW)):
                            if j == 0:
                                pe.wait_ge(ready, cut_before + half + 1)
                            for c in range(4 * half, 4 * half + 4):
                                if j == 0 and wait_x:
                                    wait_x(c)
                                for wp, xp in parts:
                                    w, x = cut[:, k, wp, c, :], x_part[xp][:, c, :]
                                    s_, m_ = (w[:, j * P:(j + 1) * P], x) if transposed else (x[:, j * P:(j + 1) * P], w)
                                    last = nc.tensor.matmul(bank(b, j * T, T), s_, m_, start=(c == 0 and wp + xp == 0),
                                                            stop=(c == DC - 1 and wp == 1))
                return last

            pe.wait_ge(s_xhi, TT)
            pe.wait_ge(s_xlo, TT)
            with pe.Fori(0, GROUPS) as g:
                for n in range(6):
                    pe.wait_ge(s_evac, 6 * g + n + 1)
                    project_cut(n % 2, n % 2, n < 4, 12 * g + 2 * n).then_inc(s_unit, 1)

            def scores(i, u):
                pe.wait_ge(s_stage, 2 * i + u + 1)
                pe.wait_ge(s_scread, FREE + 2 * i + u)
                for g in range(GROUPS):
                    nc.tensor.matmul(ps[:, 2 * 512 + g * T:2 * 512 + (g + 1) * T], stage_q[:, u, g, P:T],
                                     qk[:, 1, g, bass.ds(i, 1), :], start=True, stop=True)
                for g in range(GROUPS):
                    last = nc.tensor.matmul(bank(4, g * P, P), stage_q[:, u, g, 0:P],
                                            qk[:, 1, g, bass.ds(i, 1), 0:P], start=True, stop=True)
                last.then_inc(s_score, 1)

            def turn_probs(i, u):
                pe.wait_ge(s_prob, 2 * (2 * i + u) + 2)
                pe.wait_ge(s_ya, FREE + 2 * i + u)
                for b in range(BLOCKS):
                    last = nc.tensor.transpose(bank(5, b * P, P), prob[:, b * P:(b + 1) * P], ident)
                last.then_inc(s_ptp, 1)

            def attend(i, u):
                pe.wait_ge(s_pt, 2 * i + u + 1)
                for tt, (b0, kts) in enumerate(((2 * GROUPS, 1), (0, 2))):
                    for g in range(GROUPS):
                        for kt in range(kts):
                            last = nc.tensor.matmul(
                                bank(7, 256 + tt * HD, HD), probT[:, b0 + g * kts + kt, :],
                                v[:, g, kt, bass.ds(2 * HD * i + u * HD, HD)],
                                start=(g == 0 and kt == 0), stop=(g == GROUPS - 1 and kt == kts - 1))
                last.then_inc(s_pv, 1)

            def unit(i, n, k):
                if n == 4:
                    pe.wait_ge(s_xc, i + 1)
                elif n == 3:
                    pe.wait_ge(s_evac, 2 + UNITS_A + 4 * i + 2)
                else:
                    pe.wait_ge(s_evac, 2 + UNITS_A + 4 * i - 1 + n)
                project_cut(k, k, True, 2 * (UNITS_A + 5 * i + n)).then_inc(s_unit, 1)

            pe.wait_ge(s_evac, 2 + UNITS_A - 2)
            with pe.Fori(0, PAIRS // 2) as ii:
                for q in range(2):
                    i = 2 * ii + q
                    scores(i, 0)
                    unit(i, 0, q)
                    turn_probs(i, 0)
                    scores(i, 1)
                    unit(i, 1, 1 - q)
                    attend(i, 0)
                    unit(i, 2, q)
                    turn_probs(i, 1)
                    unit(i, 3, 1 - q)
                    attend(i, 1)
                    unit(i, 4, q)

            def unit_cd(m, b, transposed, x, wait_x=None):
                project_cut(b, m % 2, transposed, 2 * m, x, wait_x).then_inc(s_unit, 1)

            pe.wait_ge(s_ya, FREE + HEADS)
            pe.wait_ge(s_scread, FREE + HEADS)
            for j in range(4):
                for tt in range(TT):
                    last = nc.tensor.transpose(bank(2, j * T + tt * P, P), ya[:, tt, j * P:(j + 1) * P], ident)
            last.then_inc(s_yat, 1)
            pe.wait_ge(s_yahi, 1)
            pe.wait_ge(s_yalo, 1)
            for m in range(U_ATTN, U_CONV):
                pe.wait_ge(s_lo, 2 * m + 2)
                for j in range(4):
                    for c in range(4):
                        for wp, xp in PARTS:
                            last = nc.tensor.matmul(
                                bank(4 + 2 * (m - U_ATTN), j * T, T),
                                wide_piece(cut[:, m % 2, wp, :, :])[:, c, j * P:(j + 1) * P], ya_part[xp][:, c, :],
                                start=(c == 0 and wp + xp == 0), stop=(c == 3 and wp == 1))
                last.then_inc(s_unit, 1)
            pe.wait_ge(s_ychi, 1)
            pe.wait_ge(s_yclo, 1)
            pe.wait_ge(s_evac, COPIED_B)
            for n in range(4):
                if n >= 2:
                    pe.wait_ge(s_mixread, 2 + n - 1)
                if n == 2:
                    pe.wait_ge(s_mixread, 2)
                    turn_normed(1)
                unit_cd(U_CONV + n, n % 2, True, yc_part)
            for n in range(4):
                if n >= 2:
                    pe.wait_ge(s_h, n - 1)
                unit_cd(U_OUT + n, 2 + n % 2, False, mix_part,
                        None if n else lambda c: pe.wait_ge(s_mixlo, c // 2 + 1))
            pe.wait_ge(s_memhi, 1)
            pe.wait_ge(s_memlo, 1)
            for n in range(4):
                if n < 2:
                    pe.wait_ge(s_mixread, 5 + n)
                else:
                    pe.wait_ge(s_evac, COPIED_B + n - 1)
                if n == 2:
                    turn_normed(2)
                unit_cd(U_CKV + n, n % 2, n < 2, mem_part)

            pe.wait_ge(s_x2hi, TT)
            pe.wait_ge(s_x2lo, 1)
            pe.wait_ge(s_h, 2 * TT)
            for n in range(2):
                unit_cd(U_CQ + n, 2 + n, True, x2_part)
            pe.wait_ge(s_evac, COPIED_B + 6)
            for tt in range(TT):
                for m in range(MH):
                    last = nc.tensor.matmul(bank(2 + 2 * tt, m * T, T), qcT[:, m, tt * P:(tt + 1) * P], kmT[:, m, :],
                                            start=True, stop=True)
                last.then_inc(s_cs, 1)
            for tt in range(TT):
                pe.wait_ge(s_cn, tt + 1)
                for m in range(MH):
                    for b in range(TT):
                        last = nc.tensor.transpose(bank((6, 2)[tt], (m * TT + b) * P, P),
                                                   pc[:, tt, m, b * P:(b + 1) * P], ident)
                last.then_inc(s_ct, 1)
            for tt in range(TT):
                pe.wait_ge(s_cpt, tt + 1)
                for m in range(MH):
                    for b in range(TT):
                        last = nc.tensor.matmul(bank(tt, m * P, P), vm[:, b, m * MHD:(m + 1) * MHD],
                                                pcT[:, tt, m, b, :], start=(b == 0), stop=(b == TT - 1))
                last.then_inc(s_cv, 1)
            pe.wait_ge(s_co, 16)
            for tt in range(TT):
                pe.wait_ge(s_co_t, tt + 1)
                for half in range(2):
                    for m in range(MH):
                        last = nc.tensor.matmul(bank(4 + 2 * tt + half), ocT[:, tt, m, :],
                                                rows(2)[:, m, half * 512:(half + 1) * 512],
                                                start=(m == 0), stop=(m == MH - 1))
                    last.then_inc(s_hp, 1)

            pe.wait_ge(s_h, 2 * 2 * TT)
            for tt in range(TT):
                for half in range(2):
                    last = nc.tensor.matmul(bank(2 * tt + half), ident, h[:, tt, half * 512:(half + 1) * 512],
                                            start=True, stop=False, skip_group_check=True)
            turn_normed(3)
            pe.wait_ge(s_xT, 4 * TT)
            pe.wait_ge(s_wr, 48)
            for tt in range(TT):
                for c in range(DC):
                    last = nc.tensor.matmul(bank(6, tt * E, E), xT[:, c, tt * P:(tt + 1) * P], wr[:, c, :],
                                            start=(c == 0), stop=(c == DC - 1))
            last.then_inc(s_lg, 1)
            pe.wait_ge(s_sel, TT)
            before, ones = const[:, C_BEFORE:C_BEFORE + P], const[:, C_ONES:C_ONES + P]
            nc.tensor.matmul(bank(7, 0, E), before, chosen[:, 0, :], start=True, stop=True)
            nc.tensor.matmul(bank(7, E, E), ones, chosen[:, 0, :], start=True, stop=False)
            nc.tensor.matmul(bank(7, E, E), before, chosen[:, 1, :], start=False, stop=True)
            nc.tensor.matmul(bank(7, 2 * E, E), ones, chosen[:, 0, :], start=True, stop=False)
            nc.tensor.matmul(bank(7, 2 * E, E), ones, chosen[:, 1, :], start=False, stop=True).then_inc(s_pos, 1)

            def gather(count):
                pe.wait_ge(s_pick, 2 * count)
                for c in range(DC):
                    for tt in range(TT):
                        last = nc.tensor.matmul(bank(6, c * SLOTS, SLOTS), normed[:, tt, c * P:(c + 1) * P],
                                                pick[:, tt, :], start=(tt == 0), stop=(tt == TT - 1))
                last.then_inc(s_gat, 1)

            def wide(b, k0, w, fours, w0, row):
                for half in range(2 if row is not None else 0):
                    nc.tensor.matmul(bank(b)[half * SLOTS:(half + 1) * SLOTS, :],
                                     const[:, C_PICK + row * SLOTS:C_PICK + (row + 1) * SLOTS],
                                     bias[w % 2][:, half * 512:(half + 1) * 512], start=True, stop=False)
                for part in range(2):
                    s, landed = part_place(w, k0 + part, fours)
                    pe.wait_ge(s_slot[s], 16 * landed)
                    for j in range(4):
                        for half in range(2):
                            last = nc.tensor.matmul(bank(b)[half * SLOTS:(half + 1) * SLOTS, :],
                                                    w0(part, j), rows(s)[:, j, half * 512:(half + 1) * 512],
                                                    start=(row is None and part == 0 and j == 0),
                                                    stop=(part == 1 and j == 3))
                    if part == 0:
                        last.then_inc(s_half, 1)
                return last

            def add_rows(final=False):
                for tt in range(TT):
                    for half in range(2):
                        rs = slice(half * SLOTS, (half + 1) * SLOTS)
                        last = nc.tensor.matmul(bank(2 * tt + half), spreadT[rs, tt, :], y_sb[rs, :],
                                                start=False, stop=False, skip_group_check=True)
                    if final:
                        last.then_inc(s_sum, 1)

            def expert_body(w, fours, count, gathers):
                pe.wait_ge(s_xg, gathers)
                pe.wait_ge(s_bias[w % 2], 64 * fours + 32 * (w // 2 + 1))
                pe.wait_ge(s_sprT, count)
                wide(4, 0, w, fours, lambda part, j: xg[:, 4 * part + j, :], 0).then_inc(s_gate, 1)
                gather(gathers + 1)
                wide(5, 2, w, fours, lambda part, j: xg[:, 4 * part + j, :], 1).then_inc(s_up, 1)
                pe.wait_ge(s_ysb, count)
                add_rows()
                pe.wait_ge(s_hdn, count)
                pe.wait_ge(s_xg, gathers + 1)
                for j in range(4):
                    last = nc.tensor.transpose(bank(6, j * P, P),
                                               hdn.rearrange("p (n j) -> p j n", j=4)[:, j, :], ident)
                last.then_inc(s_ht, 1)
                pe.wait_ge(s_spr, 2 * count)
                pe.wait_ge(s_g, count)
                for tt in range(TT):
                    last = nc.tensor.transpose(bank(4, tt * P, P), spread[:, tt, :], ident)
                last.then_inc(s_sprt, 1)
                pe.wait_ge(s_hT, count)
                wide(7, 4, w, fours, lambda part, j: hdnT[:, j, part * SLOTS:(part + 1) * SLOTS], None).then_inc(s_y, 1)

            def last_rows(count):
                pe.wait_ge(s_sprT, FREE + count)
                pe.wait_ge(s_ysb, FREE + count)

            gather(1)
            pe.wait_ge(s_w, 1)
            for tt in range(TT):
                last = nc.tensor.transpose(bank(4, tt * P, P), spread[:, tt, :], ident)
            last.then_inc(s_sprt, 1)
            pe.wait_ge(s_bd, 32)
            with pe.Fori(0, E // 4) as i:
                for w in range(4):
                    expert_body(w, i, 4 * i + w + 1, 4 * i + w + 1)
            last_rows(E)
            pe.wait_ge(s_rounds, 1)
            rounds = pe.value_load(rounds_i[0:1, 0:1], min_val=1, max_val=T // SLOTS)
            with pe.If(rounds > 1):
                with pe.Fori(1, rounds) as r:
                    gather((E + 1) * r + 1)
                    with pe.Fori(0, E // 4) as i:
                        for w in range(4):
                            expert_body(w, E // 4 * r + i, E * r + 4 * i + w + 1, (E + 1) * r + 4 * i + w + 1)
                    last_rows(E * r + E)
            add_rows(final=True)

        @block.scalar
        def _(act):
            act.nop().then_inc(s_evac, 2)
            act.nop().then_inc(s_ysb, FREE)

            def load_sqrt_table():
                nc.scalar.activation(warm[:, 1:2], warm[:, 0:1], ACT.Sqrt).then_inc(s_table, 1)

            def sumsq_std(k, src, wait=None):
                for tt in range(TT):
                    if wait:
                        wait(tt)
                    nc.scalar.activation(normed[:, tt, :], src(tt), ACT.Square,
                                         accum_out=sumsq[:, tt:tt + 1]).then_inc(s_sq, 1)
                act.wait_ge(s_var, k + 1)
                nc.scalar.activation(std, var, ACT.Sqrt).then_inc(s_std, 1)

            def copy_unit(n, dst, src):
                act.wait_ge(s_unit, 2 + n)
                nc.scalar.copy(dst, src).then_inc(s_evac, 1)

            two = "p (a t) -> p a t"
            def evac_a(g, n):
                act.wait_ge(s_unit, 2 + 6 * g + n + 1)
                if n < 4:
                    dst = qk[:, n // 2, bass.ds(g, 1), 2 * (n % 2):2 * (n % 2) + 2, :]
                    src = bank(n % 2).rearrange("p (g a t) -> p g a t", g=1, a=2)
                else:
                    dst = v[:, bass.ds(g, 1), :, (n - 4) * 256:(n - 3) * 256]
                    src = bank(n % 2).rearrange("p (g a n) -> p g a n", g=1, a=2)
                nc.scalar.copy(dst, src).then_inc(s_evac, 1)

            act.wait_ge(s_warm, 1)
            load_sqrt_table()
            act.wait_ge(s_x, 16)
            sumsq_std(0, lambda tt: h[:, tt, :])
            for tt in range(TT):
                act.wait_ge(s_xT, tt + 1)
                nc.scalar.copy(xT_hi[:, :, tt * P:(tt + 1) * P], x_whole[:, :, tt * P:(tt + 1) * P]).then_inc(s_xhi, 1)

            def high(k, src):
                for half in range(2):
                    cs = slice(4 * half, 4 * half + 4)
                    nc.scalar.copy(cut[:, k, 0, cs, :], src[:, cs, :]).then_inc(s_hi, 1)

            act.wait_ge(s_land[0], 16)
            high(0, land[0])
            with act.Fori(0, GROUPS) as g:
                for n in range(6):
                    act.wait_ge(s_land[(n + 1) % 6], 16 * g + 16 * (1 + (n + 1) // 6))
                    act.wait_ge(s_unit, 2 + 6 * g + n)
                    high((n + 1) % 2, land[(n + 1) % 6])
                    evac_a(g, n)
            def exps(i, u):
                act.wait_ge(s_nmax, 2 * i + u + 1)
                for tt, cs in ((0, slice(KEYS1, SCORES)), (1, slice(0, KEYS1))):
                    nc.scalar.activation(prob[:, cs], prob[:, cs], ACT.Exp, bias=nmax[:, u, tt:tt + 1],
                                         scale=HD ** -0.5, accum_out=psum_[:, u, tt:tt + 1]).then_inc(s_prob, 1)

            def copy_probs(i, u):
                act.wait_ge(s_ptp, 2 * i + u + 1)
                nc.scalar.copy(probT[:, :, :], ps[:, 5 * 512:5 * 512 + SCORES].rearrange("p (b q) -> p b q", q=P))\
                    .then_inc(s_pt, 1)

            def high_b(i, n, k):
                act.wait_ge(s_land[n % 5], 16 * i + 16 * (GROUPS + 1 + n // 5))
                act.wait_ge(s_unit, 2 + UNITS_A + 5 * i + n - 1)
                high(k, land[n % 5])

            def gate(i, b, k):
                act.wait_ge(s_unit, 2 + UNITS_A + 5 * i + 4 + b)
                for j in range(2):
                    ins = nc.scalar.activation(gates[:, b, bass.ds(2 * i + j, 1), :],
                                               bank(k, j * T, T).rearrange("p (a t) -> p a t", a=1),
                                               ACT.Sigmoid, bias=vecs[:, bass.ds(V_BGATE + b * DC + j + 2 * i, 1)])
                ins.then_inc(s_evac, 1)

            with act.Fori(0, PAIRS // 2) as ii:
                for q in range(2):
                    i = 2 * ii + q
                    high_b(i, 1, 1 - q)
                    exps(i, 0)
                    high_b(i, 2, q)
                    copy_probs(i, 0)
                    act.wait_ge(s_conv, FREE + i)
                    copy_unit(UNITS_A + 5 * i + 1, gb_sb, bank(q).rearrange(two, a=2))
                    high_b(i, 3, 1 - q)
                    exps(i, 1)
                    copy_unit(UNITS_A + 5 * i + 2, gc_sb[:, :, :], bank(1 - q).rearrange(two, a=2))
                    high_b(i, 4, q)
                    copy_probs(i, 1)
                    if q == 0:
                        high_b(i, 5, 1)
                    else:
                        high_b(i, 5, 0)
                    gate(i, 0, 1 - q)
                    gate(i, 1, q)
            def high_cd(m):
                n = m - UNITS_B
                act.wait_ge(s_land[n % 4], 16 * (GROUPS + PAIRS + 1 + n // 4))
                act.wait_ge(s_unit, 2 + m - 1)
                high(m % 2, land[n % 4])

            def mix_high(n):
                act.wait_ge(s_mix, n + 1)
                nc.scalar.copy(mix_part[0][:, 2 * n:2 * n + 2, :], mixT[:, 2 * n:2 * n + 2, :]).then_inc(s_mixhi, 1)

            act.wait_ge(s_yat, 1)
            nc.scalar.copy(ya_part[0][:, :, :], ps[:, 2 * 512:4 * 512].rearrange("p (j t) -> p j t", j=4)).then_inc(s_yahi, 1)
            high_cd(U_ATTN + 1)
            act.wait_ge(s_conv, FREE + PAIRS)
            nc.scalar.copy(yc_part[0][:, :, :], ycT[:, :, :]).then_inc(s_ychi, 1)
            high_cd(U_CONV)
            act.wait_ge(s_mem, 16)
            sumsq_std(1, lambda tt: mem_in[:, tt, :])
            high_cd(U_CONV + 1)
            high_cd(U_CONV + 2)
            mix_high(0)
            high_cd(U_CONV + 3)
            mix_high(1)
            high_cd(U_OUT)
            mix_high(2)
            mix_high(3)
            high_cd(U_OUT + 1)
            act.wait_ge(s_xT, 2 * TT)
            act.wait_ge(s_mixread, 6)
            nc.scalar.copy(mem_part[0][:, :, :], memT).then_inc(s_memhi, 1)
            for m in range(U_OUT + 2, U_CKV + 2):
                high_cd(m)
            act.wait_ge(s_h, 2 * TT)
            act.wait_ge(s_trn, 2 * TT)
            sumsq_std(2, lambda tt: h[:, tt, :])
            high_cd(U_CKV + 2)
            copy_unit(U_CKV + 1, kmT[:, 0:2, :], bank(0).rearrange(two, a=2))
            high_cd(U_CKV + 3)
            copy_unit(U_CKV + 2, kmT[:, 2:4, :], bank(1).rearrange(two, a=2))
            for tt in range(TT):
                act.wait_ge(s_xT, 2 * TT + tt + 1)
                ts = slice(tt * P, (tt + 1) * P)
                nc.scalar.copy(x2_part[0][:, :, ts], x2[:, :, ts]).then_inc(s_x2hi, 1)
            high_cd(U_CQ)
            copy_unit(U_CKV + 3, vm[:, :, 0:256], bank(0).rearrange(two, a=2))
            high_cd(U_CQ + 1)
            copy_unit(U_CKV + 4, vm[:, :, 256:512], bank(1).rearrange(two, a=2))
            for j in range(2):
                copy_unit(U_CQ + 1 + j, qcT[:, 2 * j:2 * j + 2, :], bank(2 + j).rearrange(two, a=2))
            for tt in range(TT):
                act.wait_ge(s_cm, tt + 1)
                for m in range(MH):
                    nc.scalar.activation(pc[:, tt, m, :], bank(2 + 2 * tt, m * T, T), ACT.Exp,
                                         bias=cneg[:, tt, m:m + 1], scale=MHD ** -0.5,
                                         accum_out=csum[:, tt, m:m + 1]).then_inc(s_ce, 1)
            for tt in range(TT):
                act.wait_ge(s_ct, tt + 1)
                nc.scalar.copy(pcT[:, tt, :, :, :], bank((6, 2)[tt], 0, 1024)
                               .rearrange("p (m b t) -> p m b t", m=MH, b=TT)).then_inc(s_cpt, 1)
            for tt in range(TT):
                act.wait_ge(s_cv, tt + 1)
                nc.scalar.copy(ocT[:, tt, :, :], bank(tt).rearrange("p (m t) -> p m t", m=MH)).then_inc(s_co_t, 1)
            load_sqrt_table()
            act.wait_ge(s_h, 4 * TT)
            sumsq_std(3, lambda tt: h[:, tt, :])
            act.dma_start(g_fin, io["norm_final"].rearrange("(a d) -> a d", a=1).to_broadcast([P, D])).then_inc(s_gfin, 16)
            act.wait_ge(s_top, 1)
            for tt in range(TT):
                nc.scalar.activation(gate_w[:, tt, :], logit[:, tt, 0:E], ACT.Exp,
                                     bias=topneg[:, tt:tt + 1]).then_inc(s_ex, 1)
            act.wait_ge(s_sprt, 1)
            nc.scalar.copy(spreadT, bank(4, 0, TT * P).rearrange("p (a t) -> p a t", a=TT)).then_inc(s_sprT, 1)

            def expert_body(count):
                act.wait_ge(s_g, count)
                nc.scalar.activation(act_s, act_g, ACT.Sigmoid, scale=ALPHA).then_inc(s_sig, 1)
                act.wait_ge(s_ht, count)
                nc.scalar.copy(hdnT, bank(6).rearrange("p (j s) -> p j s", j=4)).then_inc(s_hT, 1)
                act.wait_ge(s_sprt, FREE + count)
                nc.scalar.copy(spreadT, bank(4, 0, TT * P).rearrange("p (a t) -> p a t", a=TT)).then_inc(s_sprT, 1)
                act.wait_ge(s_y, count)
                nc.scalar.copy(y_sb, bank(7)).then_inc(s_ysb, 1)

            with act.Fori(0, E // 2) as i:
                for u in range(2):
                    expert_body(2 * i + u + 1)
            act.wait_ge(s_rounds, 1)
            rounds = act.value_load(rounds_i[0:1, 0:1], min_val=1, max_val=T // SLOTS)
            with act.If(rounds > 1):
                with act.Fori(1, rounds) as r:
                    with act.Fori(0, E // 2) as i:
                        for u in range(2):
                            expert_body(E * r + 2 * i + u + 1)
            load_sqrt_table()
            sumsq_std(4, lambda tt: bank(2 * tt, 0, D), lambda tt: act.wait_ge(s_sum, tt + 1))

        @block.vector
        def _(dve):
            steps = [0]

            def link(ins):
                steps[0] += 1
                ins.then_inc(s_dve, 1)
                dve.wait_ge(s_dve, steps[0])

            def norm(k, src, permuted=False):
                dve.wait_ge(s_sq, TT * (k + 1))
                nc.vector.tensor_scalar(var, sumsq, 1.0 / D, EPS, ALU.mult, ALU.add).then_inc(s_var, 1)
                dve.wait_ge(s_std, k + 1)
                link(nc.vector.reciprocal(rstd, std))
                for tt in range(TT):
                    dst, x = normed[:, tt, :], src(tt)
                    if permuted:
                        dst = dst.rearrange("t (c p) -> t c p", c=DC)
                        x = x.rearrange("t (p c) -> t c p", c=DC)
                    nc.vector.tensor_scalar(dst, x, rstd[:, tt:tt + 1], None, ALU.mult).then_inc(s_nrm, 1)

            def gained(k, dst, gain):
                for tt in range(TT):
                    dve.wait_ge(s_trn, TT * k + tt + 1)
                    nc.vector.tensor_tensor(dst[:, :, tt * P:(tt + 1) * P],
                                            bank(4 + 2 * tt, 0, D).rearrange("p (c t) -> p c t", c=DC),
                                            gain.rearrange("p (c o) -> p c o", o=1).to_broadcast([P, DC, P]),
                                            ALU.mult).then_inc(s_xT, 1)

            dve.nop().then_inc(s_scread, FREE)
            dve.nop().then_inc(s_ya, FREE)
            dve.nop().then_inc(s_conv, FREE)
            dve.wait_ge(s_vecT, 1)
            link(nc.vector.tensor_copy(vecs[:, :], bank(2, 0, V_ALL)))
            norm(0, lambda tt: h[:, tt, :])
            gained(0, x_whole, vecs[:, V_MIX:V_MIX + DC])
            for tt in range(TT):
                ts = slice(tt * P, (tt + 1) * P)
                dve.wait_ge(s_xhi, tt + 1)
                nc.vector.tensor_tensor(xT_lo[:, :, ts], x_whole[:, :, ts], xT_hi[:, :, ts].bitcast(F32), ALU.subtract)\
                    .then_inc(s_xlo, 1)

            def low(k, src, m):
                for half in range(2):
                    cs = slice(4 * half, 4 * half + 4)
                    dve.wait_ge(s_hi, 2 * m + half + 1)
                    nc.vector.tensor_tensor(cut[:, k, 1, cs, :], src[:, cs, :], cut[:, k, 0, cs, :].bitcast(F32),
                                            ALU.subtract).then_inc(s_lo, 1)

            low(0, land[0], 0)
            with dve.Fori(0, GROUPS) as g:
                for n in range(6):
                    low((n + 1) % 2, land[(n + 1) % 6], 6 * g + n + 1)

            def soft(i, u, n):
                dve.wait_ge(s_score, 2 + 2 * i + u + 1)
                slope = const[:, bass.ds(C_SLOPE + u + 2 * i, 1)]
                for cs, b in ((slice(0, KEYS1), 2), (slice(KEYS1, SCORES), 4)):
                    ins = nc.vector.scalar_tensor_tensor(
                        out=prob[:, cs], in0=const[:, C_DIST + cs.start:C_DIST + cs.stop], scalar=slope,
                        in1=bank(b, 0, cs.stop - cs.start), op0=ALU.mult, op1=ALU.add)
                ins.then_inc(s_scread, 1)
                dve.wait_ge(s_scread, FREE + 2 * i + u + 1)
                for tt, cs in ((0, slice(KEYS1, SCORES)), (1, slice(0, KEYS1))):
                    ins = nc.vector.tensor_reduce(rowmax[:, tt:tt + 1], prob[:, cs], AX_X, ALU.max)
                n(ins)
                nc.vector.tensor_scalar(nmax[:, u, :], rowmax, -HD ** -0.5, None, ALU.mult).then_inc(s_nmax, 1)

            def take_out(i, u, n):
                dve.wait_ge(s_prob, 2 * (2 * i + u) + 2)
                n(nc.vector.reciprocal(rinv[:, u, :], psum_[:, u, :]))
                dve.wait_ge(s_pv, 2 * i + u + 1)
                for tt in range(TT):
                    ins = nc.vector.tensor_scalar(ya[:, tt, bass.ds(2 * HD * i + u * HD, HD)],
                                                  bank(7, 256 + tt * HD, HD), rinv[:, u, tt:tt + 1], None, ALU.mult)
                ins.then_inc(s_ya, 1)

            dve.wait_ge(s_const, 16)
            dve.wait_ge(s_zero, 5)
            base, per = steps[0], 7
            with dve.Fori(0, PAIRS // 2) as ii:
                for q in range(2):
                    i = 2 * ii + q
                    k = [0]

                    def n(ins):
                        k[0] += 1
                        ins.then_inc(s_dve, 1)
                        dve.wait_ge(s_dve, base + per * i + k[0])

                    soft(i, 0, n)
                    low(1 - q, land[1], UNITS_A + 5 * i + 1)
                    low(q, land[2], UNITS_A + 5 * i + 2)
                    soft(i, 1, n)
                    take_out(i, 0, n)
                    low(1 - q, land[3], UNITS_A + 5 * i + 3)
                    dve.wait_ge(s_unit, 2 + UNITS_A + 5 * i + 3)
                    dve.wait_ge(s_evac, 2 + UNITS_A + 4 * i + 2)
                    nc.vector.tensor_tensor(conv_z[:, :, CONV_K - 1:], bank(q).rearrange("p (a t) -> p a t", a=2),
                                            gc_sb[:, :, :], ALU.mult).then_inc(s_xc, 1)
                    low(q, land[4], UNITS_A + 5 * i + 4)
                    dve.wait_ge(s_xc, i + 1)
                    for tap in range(CONV_K):
                        for j in range(2):
                            w = vecs[:, bass.ds(V_CONV + tap * DC + j + 2 * i, 1)]
                            z = conv_z[:, j:j + 1, tap:tap + T]
                            y = ycT[:, bass.ds(2 * i + j, 1), :]
                            if tap == 0:
                                ins = nc.vector.tensor_scalar(y, z, w, None, ALU.mult)
                            else:
                                ins = nc.vector.scalar_tensor_tensor(out=y, in0=z, scalar=w, in1=y,
                                                                     op0=ALU.mult, op1=ALU.add)
                        n(ins)
                    nc.vector.tensor_tensor(ycT[:, bass.ds(2 * i, 2), :], ycT[:, bass.ds(2 * i, 2), :], gb_sb, ALU.mult)\
                        .then_inc(s_conv, 1)
                    take_out(i, 1, n)
                    assert k[0] == per
                    if q == 0:
                        low(1, land[0], UNITS_A + 5 * i + 5)
                    else:
                        low(0, land[0], UNITS_A + 5 * i + 5)
            steps[0] += per * PAIRS

            def low_cd(m):
                low(m % 2, land[(m - UNITS_B) % 4], m)

            def rest(part, whole, high_ready, count, out):
                dve.wait_ge(high_ready, count)
                nc.vector.tensor_tensor(part[1], whole, part[0].bitcast(F32), ALU.subtract).then_inc(out, 1)

            def attn_branch(n):
                dve.wait_ge(s_unit, 2 + U_ATTN + n + 1)
                nc.vector.tensor_tensor(mixT[:, 4 * n:4 * n + 4, :], bank(4 + 2 * n, 0, 4 * T).rearrange("p (c t) -> p c t", c=4),
                                        gates[:, 0, 4 * n:4 * n + 4, :], ALU.mult).then_inc(s_mixread, 1)

            def conv_branch(n):
                two = slice(2 * n, 2 * n + 2)
                dve.wait_ge(s_unit, 2 + U_CONV + n + 1)
                nc.vector.tensor_tensor(mix_b, bank(n % 2).rearrange("p (c t) -> p c t", c=2),
                                        gates[:, 1, two, :], ALU.mult).then_inc(s_mixread, 1)
                dve.wait_ge(s_mixread, 2 + n + 1)
                nc.vector.tensor_tensor(mixT[:, two, :], mixT[:, two, :], mix_b, ALU.add).then_inc(s_mix, 1)
                rest([p_[:, two, :] for p_ in mix_part], mixT[:, two, :], s_mixhi, n + 1, s_mixlo)

            def add_out(n):
                dve.wait_ge(s_unit, 2 + U_OUT + n + 1)
                hh = h[:, :, n * 256:(n + 1) * 256]
                nc.vector.tensor_tensor(hh, bank(2 + n % 2).rearrange("p (a n) -> p a n", a=TT), hh, ALU.add).then_inc(s_h, 1)

            rest([p_[:, :, :] for p_ in ya_part], bank(2, 0, 4 * T).rearrange("p (j t) -> p j t", j=4), s_yahi, 1, s_yalo)
            low_cd(U_ATTN + 1)
            rest([p_[:, :, :] for p_ in yc_part], ycT[:, :, :], s_ychi, 1, s_yclo)
            low_cd(U_CONV)
            attn_branch(0)
            norm(1, lambda tt: mem_in[:, tt, :])
            low_cd(U_CONV + 1)
            attn_branch(1)
            low_cd(U_CONV + 2)
            conv_branch(0)
            low_cd(U_CONV + 3)
            conv_branch(1)
            gained(1, memT, vecs[:, V_MEM:V_MEM + DC])
            low_cd(U_OUT)
            conv_branch(2)
            conv_branch(3)
            low_cd(U_OUT + 1)
            rest([p_[:, :, :] for p_ in mem_part], memT, s_memhi, 1, s_memlo)
            for n in range(4):
                add_out(n)
                low_cd(U_OUT + 2 + n)
            dve.wait_ge(s_h, 2 * TT)
            norm(2, lambda tt: h[:, tt, :])
            low_cd(U_CKV + 2)
            low_cd(U_CKV + 3)
            gained(2, x2, vecs[:, V_CROSS:V_CROSS + DC])
            rest([p_[:, :, :] for p_ in x2_part], x2, s_x2hi, TT, s_x2lo)
            low_cd(U_CQ)
            low_cd(U_CQ + 1)
            for tt in range(TT):
                dve.wait_ge(s_cs, tt + 1)
                link(nc.vector.tensor_reduce(cmax[:, tt, :], bank(2 + 2 * tt, 0, MH * T)
                                             .rearrange("p (m k) -> p m k", m=MH), AX_X, ALU.max))
                nc.vector.tensor_scalar(cneg[:, tt, :], cmax[:, tt, :], -MHD ** -0.5, None, ALU.mult).then_inc(s_cm, 1)
            for tt in range(TT):
                dve.wait_ge(s_ce, MH * (tt + 1))
                link(nc.vector.reciprocal(cinv[:, tt, :], csum[:, tt, :]))
                nc.vector.tensor_tensor(pc[:, tt, :, :], pc[:, tt, :, :],
                                        cinv[:, tt, :].rearrange("p (m o) -> p m o", o=1).to_broadcast([P, MH, T]),
                                        ALU.mult).then_inc(s_cn, 1)
            for tt in range(TT):
                for half in range(2):
                    dve.wait_ge(s_hp, 2 * tt + half + 1)
                    hh = h[:, tt, half * 512:(half + 1) * 512]
                    nc.vector.tensor_tensor(hh, bank(4 + 2 * tt + half), hh, ALU.add).then_inc(s_h, 1)
            slots1, slots2 = const[:, C_SLOT:C_SLOT + SLOTS], const[:, C_SLOT:C_SLOT + 2 * SLOTS]

            def picks(e):
                for tt in range(TT):
                    nc.vector.tensor_scalar(pick[:, tt, :], slots1, place[:, tt, bass.ds(e, 1)], None, ALU.is_equal)\
                        .then_inc(s_pick, 1)

            dve.wait_ge(s_h, 4 * TT)
            norm(3, lambda tt: h[:, tt, :], permuted=True)
            dve.wait_ge(s_wr, 48)
            gained(3, xT, g_moe[:, :])
            dve.wait_ge(s_lg, 1)
            for tt in range(TT):
                ins = nc.vector.tensor_tensor(logit[:, tt, 0:E], bank(6, tt * E, E), rb[:, :], ALU.add)
            link(ins)
            for tt in range(TT):
                ins = nc.vector.max(top8[:, tt, :], logit[:, tt, 0:E])
            link(ins)
            nc.vector.tensor_scalar(topneg, top8[:, :, 0], -1.0, None, ALU.mult).then_inc(s_top, 1)
            link(nc.vector.tensor_copy(wanted[:, :, 0:TOPK], top8[:, :, 0:TOPK]))
            for tt in range(TT):
                ins = nc.vector.match_replace(out=logit_r[:, tt, :], in_to_replace=wanted[:, tt, :],
                                              in_values=logit[:, tt, :], imm_value=TAKEN)
            link(ins)
            for tt in range(TT):
                nc.vector.tensor_tensor(chosen[:, tt, :], logit_r[:, tt, 0:E], logit[:, tt, 0:E], ALU.is_lt)\
                    .then_inc(s_sel, 1)
            dve.wait_ge(s_sel, TT)
            dve.wait_ge(s_ex, TT)
            link(nc.vector.tensor_tensor(gate_w[:, :, :], gate_w[:, :, :], chosen[:, :, :], ALU.mult))
            link(nc.vector.tensor_reduce(topsum, gate_w[:, :, :], AX_X, ALU.add))
            link(nc.vector.reciprocal(topinv, topsum))
            for tt in range(TT):
                ins = nc.vector.tensor_scalar(gate_w[:, tt, :], gate_w[:, tt, :], topinv[:, tt:tt + 1], None, ALU.mult)
            link(ins)
            dve.wait_ge(s_pos, 1)
            for tt in range(TT):
                ins = nc.vector.scalar_tensor_tensor(out=place[:, tt, 0:E], in0=bank(7, tt * E, E), scalar=1.0,
                                                     in1=chosen[:, tt, :], op0=ALU.add, op1=ALU.mult)
            link(ins)
            link(nc.vector.tensor_scalar(place[:, :, 0:E], place[:, :, 0:E], -1.0, None, ALU.add))
            picks(0)
            dve.wait_ge(s_zero, 9)
            for half in range(2):
                ins = nc.vector.tensor_copy(spread[:, :, half * SLOTS:half * SLOTS + E], gate_w[:, :, :])
            ins.then_inc(s_w, 1)
            link(nc.vector.tensor_reduce(most, bank(7, 2 * E, E), AX_X, ALU.max))
            link(nc.vector.tensor_scalar(rounds_f[:, 0:1], most, float(SLOTS), 1.0, ALU.is_gt, ALU.add))
            for k in range(2):
                link(nc.vector.scalar_tensor_tensor(out=rounds_f[:, k + 1:k + 2], in0=most, scalar=float(SLOTS * (k + 2)),
                                                    in1=rounds_f[:, k:k + 1], op0=ALU.is_gt, op1=ALU.add))
            nc.vector.tensor_copy(rounds_i[:, :], rounds_f[:, 2:3]).then_inc(s_rounds, 1)

            def spreads(e):
                for tt in range(TT):
                    nc.vector.tensor_scalar(spread[:, tt, :], slots2, place[:, tt, bass.ds(e, 1)],
                                            gate_w[:, tt, bass.ds(e, 1)], ALU.is_equal, ALU.mult).then_inc(s_spr, 1)

            def take_gathered(gathers):
                dve.wait_ge(s_gat, gathers)
                nc.vector.tensor_tensor(xg[:, :, :], bank(6).rearrange("p (c s) -> p c s", c=DC),
                                        g_moe[:, :].rearrange("p (c o) -> p c o", o=1).to_broadcast([P, DC, SLOTS]),
                                        ALU.mult).then_inc(s_xg, 1)

            def expert_body(e, count, gathers):
                picks(e + 1)
                dve.wait_ge(s_sprt, count)
                spreads(e)
                dve.wait_ge(s_gate, count)
                nc.vector.tensor_scalar(act_g, bank(4), LIMIT, None, ALU.min).then_inc(s_g, 1)
                dve.wait_ge(s_sig, count)
                nc.vector.tensor_tensor(act_s, act_g, act_s, ALU.mult)
                dve.wait_ge(s_up, count)
                ins = nc.vector.tensor_scalar(act_l, bank(5), -LIMIT, LIMIT, ALU.max, ALU.min)
                ins.then_inc(s_lin, 1)
                dve.wait_ge(s_lin, count)
                nc.vector.scalar_tensor_tensor(out=hdn, in0=act_l, scalar=1.0, in1=act_s, op0=ALU.add, op1=ALU.mult)\
                    .then_inc(s_hdn, 1)
                take_gathered(gathers + 1)

            take_gathered(1)
            with dve.Fori(0, E // 2) as i:
                for u in range(2):
                    expert_body(2 * i + u, 2 * i + u + 1, 2 * i + u + 1)
            dve.wait_ge(s_rounds, 1)
            rounds = dve.value_load(rounds_i[0:1, 0:1], min_val=1, max_val=T // SLOTS)
            with dve.If(rounds > 1):
                with dve.Fori(1, rounds) as r:
                    nc.vector.tensor_scalar(place[:, :, :], place[:, :, :], -float(SLOTS), None, ALU.add)\
                        .then_inc(s_route, 1)
                    dve.wait_ge(s_route, r)
                    picks(0)
                    take_gathered((E + 1) * r + 1)
                    with dve.Fori(0, E // 2) as i:
                        for u in range(2):
                            expert_body(2 * i + u, E * r + 2 * i + u + 1, (E + 1) * r + 2 * i + u + 1)
            dve.wait_ge(s_sq, TT * 5)
            nc.vector.tensor_scalar(var, sumsq, 1.0 / D, EPS, ALU.mult, ALU.add).then_inc(s_var, 1)
            dve.wait_ge(s_std, 5)
            link(nc.vector.reciprocal(rstd, std))
            dve.wait_ge(s_gfin, 16)
            for tt in range(TT):
                nc.vector.scalar_tensor_tensor(out=outp[:, tt, :], in0=bank(2 * tt, 0, D), scalar=rstd[:, tt:tt + 1],
                                               in1=g_fin, op0=ALU.mult, op1=ALU.mult).then_inc(s_out, 1)


_IN = ("x", "mem", "norm_mix", "w_in", "conv_w", "w_branch_attn", "w_branch_conv", "w_gate", "b_gate", "w_out",
       "norm_cross", "norm_mem", "w_cq", "w_ckv", "w_co", "norm_moe", "router_w", "router_b",
       "w_exp_gate", "b_exp_gate", "w_exp_up", "b_exp_up", "w_exp_down", "b_exp_down", "norm_final")


def kernel(**inputs):
    import concourse.bacc as bacc
    from concourse.bass_utils import run_bass_kernel_spmd

    nc = bacc.Bacc("TRN2", target_bir_lowering=False, num_devices=1)
    arrays, io = {}, {}
    for name in _IN:
        a = np.ascontiguousarray(inputs[name])
        if name != "norm_final":
            a = a.reshape(a.shape[1:])
        if name == "conv_w":
            a = a.reshape(-1)
        arrays[f"in_{name}"] = a
    arrays["in_const"] = constants()
    for key, a in arrays.items():
        io[key[3:]] = nc.dram_tensor(key, a.shape, F32, kind="ExternalInput").ap()
    io["out"] = nc.dram_tensor("out_h", (T, D), F32, kind="ExternalOutput").ap()
    build(nc, io)
    r = run_bass_kernel_spmd(nc, [arrays], core_ids=[0])
    return r.results[0]["out_h"].reshape(inputs["x"].shape)
```
